# Optimizing a Trainium2 kernel written in Bass

```python
import math
import jax
import jax.numpy as jnp
from jax import lax
import numpy as np

D_MODEL = 1024
BATCH = 1
SEQ = 512
DEPTH = 2

GRID_W = 64
CTX_LEN = 256
N_GROUPS = 4
HEADS = 4
HEAD_DIM = D_MODEL // (N_GROUPS * HEADS)
MIX_WIDTH = N_GROUPS * HEADS * HEAD_DIM
NA_WIN_R = 8
NA_WIN_C = 16
MLA_Q_LORA = 3 * D_MODEL // 16
MLA_KV_LORA = D_MODEL // 8
MLA_NOPE = HEAD_DIM
MLA_ROPE = HEAD_DIM // 2
MLA_V = HEAD_DIM
SWA_HKV = 2
SWA_GROUP = HEADS // SWA_HKV
SWA_WINDOW = 128
DIFF_DH = HEAD_DIM // 2
D_FF = 4 * D_MODEL
BLK = 128
ROPE_BASE = 10000.0
EPS = 1e-6
NEG_INF = -1e30
IN_SIZES = (
    HEADS * HEAD_DIM, HEADS * HEAD_DIM, HEADS * HEAD_DIM,
    MLA_Q_LORA, MLA_KV_LORA, MLA_ROPE,
    HEADS * HEAD_DIM, SWA_HKV * HEAD_DIM, SWA_HKV * HEAD_DIM,
    HEADS * 2 * DIFF_DH, HEADS * 2 * DIFF_DH, HEADS * HEAD_DIM,
)
IN_COLS = sum(IN_SIZES)

kernel_name = 'hybrid_parallel_heads_dit_block'

def rmsnorm(x, g):
    xf = x.astype(jnp.float32)
    y = xf * lax.rsqrt(jnp.mean(xf * xf, axis=-1, keepdims=True) + EPS)
    return (y * g.astype(jnp.float32)).astype(x.dtype)

def modulate(h, shift, scale):
    return h * (1 + scale) + shift

def split_heads(t, n):
    return t.reshape(t.shape[:-1] + (n, t.shape[-1] // n))

def split_cols(z):
    parts, start = [], 0
    for size in IN_SIZES:
        parts.append(z[..., start:start + size])
        start += size
    return parts

def softmax_f32(s):
    return jax.nn.softmax(s.astype(jnp.float32), axis=-1)

def axial_rope(row, col, dim):
    n_freq = dim // 4
    freqs = ROPE_BASE ** (-jnp.arange(n_freq, dtype=jnp.float32) / n_freq)
    ang = jnp.concatenate([row.astype(jnp.float32)[:, None] * freqs,
                           col.astype(jnp.float32)[:, None] * freqs], axis=-1)
    return jnp.cos(ang), jnp.sin(ang)

def apply_rope(x, rope):
    cos, sin = rope
    cos = cos[:, None, :].astype(x.dtype)
    sin = sin[:, None, :].astype(x.dtype)
    half = x.shape[-1] // 2
    x1, x2 = x[..., :half], x[..., half:]
    return jnp.concatenate([x1 * cos - x2 * sin, x1 * sin + x2 * cos], axis=-1)

def sweep_query_blocks(fn, q):
    B, L = q.shape[:2]
    qb = jnp.moveaxis(q.reshape((B, L // BLK, BLK) + q.shape[2:]), 1, 0)
    o = lax.map(fn, qb)
    return jnp.moveaxis(o, 0, 1).reshape((B, L) + o.shape[3:])

def attend(q, k, v, scale):
    s = jnp.einsum('bqhd,bkhd->bhqk', q, k).astype(jnp.float32) * scale
    p = softmax_f32(s).astype(v.dtype)
    return jnp.einsum('bhqk,bkhd->bqhd', p, v)

def neighbourhood_attention(zl, zc, rpb, need_ctx):
    q, k, v = (split_heads(t, HEADS) for t in zl)
    qc, kc, vc = (split_heads(t, HEADS) for t in zc)
    B, S = q.shape[:2]
    rows_n = S // GRID_W
    kr_n = min(NA_WIN_R, rows_n)
    n_loc = kr_n * GRID_W
    scale = HEAD_DIM ** -0.5
    qg = q.reshape(B, rows_n, GRID_W, HEADS, HEAD_DIM)
    kg = k.reshape(B, rows_n, GRID_W, HEADS, HEAD_DIM)
    vg = v.reshape(B, rows_n, GRID_W, HEADS, HEAD_DIM)
    col = jnp.arange(GRID_W)
    c0 = jnp.clip(col - NA_WIN_C // 2, 0, GRID_W - NA_WIN_C)
    col_ok = (col[None, :] >= c0[:, None]) & (col[None, :] < c0[:, None] + NA_WIN_C)
    dc_idx = jnp.clip(col[None, :] - col[:, None], 1 - NA_WIN_C, NA_WIN_C - 1) + (NA_WIN_C - 1)

    def row_block(r):
        r0 = jnp.clip(r - kr_n // 2, 0, rows_n - kr_n)
        q_r = lax.dynamic_index_in_dim(qg, r, axis=1, keepdims=False)
        k_r = lax.dynamic_slice_in_dim(kg, r0, kr_n, axis=1).reshape(B, n_loc, HEADS, HEAD_DIM)
        v_r = lax.dynamic_slice_in_dim(vg, r0, kr_n, axis=1).reshape(B, n_loc, HEADS, HEAD_DIM)
        dr_idx = r0 + jnp.arange(kr_n) - r + (NA_WIN_R - 1)
        bias = rpb[:, dr_idx[None, :, None], dc_idx[:, None, :]].astype(jnp.float32)
        bias = jnp.where(col_ok[None, :, None, :], bias, NEG_INF).reshape(HEADS, GRID_W, n_loc)
        s_loc = jnp.einsum('bqhd,bkhd->bhqk', q_r, k_r).astype(jnp.float32) * scale + bias
        s_ctx = jnp.einsum('bqhd,bchd->bhqc', q_r, kc).astype(jnp.float32) * scale
        p = softmax_f32(jnp.concatenate([s_loc, s_ctx], axis=-1)).astype(v.dtype)
        return (jnp.einsum('bhqk,bkhd->bqhd', p[..., :n_loc], v_r)
                + jnp.einsum('bhqc,bchd->bqhd', p[..., n_loc:], vc))

    o = lax.map(row_block, jnp.arange(rows_n))
    o_lat = jnp.moveaxis(o, 0, 1).reshape(B, S, HEADS * HEAD_DIM)
    o_ctx = attend(qc, kc, vc, scale).reshape(B, -1, HEADS * HEAD_DIM) if need_ctx else None
    return o_lat, o_ctx

def mla_project(cq, ckv, kr, gq, w_uq, gkv, w_ukv, rope):
    q = split_heads(rmsnorm(cq, gq) @ w_uq, HEADS)
    kv = split_heads(rmsnorm(ckv, gkv) @ w_ukv, HEADS)
    q_nope, q_rope = q[..., :MLA_NOPE], q[..., MLA_NOPE:]
    k_nope, v = kv[..., :MLA_NOPE], kv[..., MLA_NOPE:]
    k_rope = kr[:, :, None, :]
    if rope is not None:
        q_rope = apply_rope(q_rope, rope)
        k_rope = apply_rope(k_rope, rope)
    q = jnp.concatenate([q_nope, q_rope], axis=-1)
    k = jnp.concatenate([k_nope, jnp.broadcast_to(k_rope, k_nope.shape[:-1] + (MLA_ROPE,))], axis=-1)
    return q, k, v

def latent_attention(zl, zc, gq, w_uq, gkv, w_ukv, rope, need_ctx):
    B, S = zl[0].shape[:2]
    ql, kl, vl = mla_project(zl[0], zl[1], zl[2], gq, w_uq, gkv, w_ukv, rope)
    qc, kc, vc = mla_project(zc[0], zc[1], zc[2], gq, w_uq, gkv, w_ukv, None)
    scale = (MLA_NOPE + MLA_ROPE) ** -0.5
    k_all = jnp.concatenate([kl, kc], axis=1)
    v_all = jnp.concatenate([vl, vc], axis=1)
    o_lat = sweep_query_blocks(lambda qi: attend(qi, k_all, v_all, scale), ql).reshape(B, S, HEADS * MLA_V)
    o_ctx = attend(qc, kc, vc, scale).reshape(B, -1, HEADS * MLA_V) if need_ctx else None
    return o_lat, o_ctx

def window_attention(zl, zc, sink, rope, need_ctx):
    B, S = zl[0].shape[:2]
    C = zc[0].shape[1]
    ql = apply_rope(split_heads(zl[0], HEADS), rope)
    kl = apply_rope(split_heads(zl[1], SWA_HKV), rope)
    vl = split_heads(zl[2], SWA_HKV)
    qc = zc[0].reshape(B, C, SWA_HKV, SWA_GROUP, HEAD_DIM)
    kc = split_heads(zc[1], SWA_HKV)
    vc = split_heads(zc[2], SWA_HKV)
    scale = HEAD_DIM ** -0.5
    sink_hg = sink.astype(jnp.float32).reshape(SWA_HKV, SWA_GROUP)
    pad = ((0, 0), (BLK, BLK), (0, 0), (0, 0))
    kp = jnp.pad(kl, pad)
    vp = jnp.pad(vl, pad)

    def band_block(i):
        q_i = lax.dynamic_slice_in_dim(ql, i * BLK, BLK, axis=1).reshape(B, BLK, SWA_HKV, SWA_GROUP, HEAD_DIM)
        k_i = lax.dynamic_slice_in_dim(kp, i * BLK, 3 * BLK, axis=1)
        v_i = lax.dynamic_slice_in_dim(vp, i * BLK, 3 * BLK, axis=1)
        qpos = i * BLK + jnp.arange(BLK)
        kpos = i * BLK - BLK + jnp.arange(3 * BLK)
        valid = ((jnp.abs(kpos[None, :] - qpos[:, None]) <= SWA_WINDOW)
                 & (kpos >= 0)[None, :] & (kpos < S)[None, :])
        s_loc = jnp.einsum('bqhgd,bkhd->bhgqk', q_i, k_i).astype(jnp.float32) * scale
        s_loc = jnp.where(valid, s_loc, NEG_INF)
        s_ctx = jnp.einsum('bqhgd,bchd->bhgqc', q_i, kc).astype(jnp.float32) * scale
        s_sink = jnp.broadcast_to(sink_hg[None, :, :, None, None], (B, SWA_HKV, SWA_GROUP, BLK, 1))
        p = softmax_f32(jnp.concatenate([s_loc, s_ctx, s_sink], axis=-1)).astype(vl.dtype)
        o = (jnp.einsum('bhgqk,bkhd->bqhgd', p[..., :3 * BLK], v_i)
             + jnp.einsum('bhgqc,bchd->bqhgd', p[..., 3 * BLK:3 * BLK + C], vc))
        return o.reshape(B, BLK, HEADS * HEAD_DIM)

    o = lax.map(band_block, jnp.arange(S // BLK))
    o_lat = jnp.moveaxis(o, 0, 1).reshape(B, S, HEADS * HEAD_DIM)
    o_ctx = None
    if need_ctx:
        s = jnp.einsum('bqhgd,bkhd->bhgqk', qc, kc).astype(jnp.float32) * scale
        s_sink = jnp.broadcast_to(sink_hg[None, :, :, None, None], (B, SWA_HKV, SWA_GROUP, C, 1))
        p = softmax_f32(jnp.concatenate([s, s_sink], axis=-1))[..., :C].astype(vc.dtype)
        o_ctx = jnp.einsum('bhgqk,bkhd->bqhgd', p, vc).reshape(B, C, HEADS * HEAD_DIM)
    return o_lat, o_ctx

def differential_attention(zl, zc, lam_params, norm_g, lam_init, rope, need_ctx):
    B, S = zl[0].shape[:2]
    C = zc[0].shape[1]
    ql = apply_rope(split_heads(zl[0], 2 * HEADS), rope).reshape(B, S, HEADS, 2, DIFF_DH)
    kl = apply_rope(split_heads(zl[1], 2 * HEADS), rope).reshape(B, S, HEADS, 2, DIFF_DH)
    vl = split_heads(zl[2], HEADS)
    qc = zc[0].reshape(B, C, HEADS, 2, DIFF_DH)
    kc = zc[1].reshape(B, C, HEADS, 2, DIFF_DH)
    vc = split_heads(zc[2], HEADS)
    lp = lam_params.astype(jnp.float32)
    lam = jnp.exp(jnp.sum(lp[0] * lp[1])) - jnp.exp(jnp.sum(lp[2] * lp[3])) + lam_init
    scale = DIFF_DH ** -0.5
    k_all = jnp.concatenate([kl, kc], axis=1)
    v_all = jnp.concatenate([vl, vc], axis=1)

    def diff_attend(q, k, v):
        s = jnp.einsum('bqhtd,bkhtd->bhtqk', q, k).astype(jnp.float32) * scale
        p = softmax_f32(s)
        a = (p[:, :, 0] - lam * p[:, :, 1]).astype(v.dtype)
        o = jnp.einsum('bhqk,bkhd->bqhd', a, v)
        return rmsnorm(o, norm_g) * (1.0 - lam_init)

    o_lat = sweep_query_blocks(lambda qi: diff_attend(qi, k_all, v_all), ql).reshape(B, S, HEADS * HEAD_DIM)
    o_ctx = diff_attend(qc, kc, vc).reshape(B, C, HEADS * HEAD_DIM) if need_ctx else None
    return o_lat, o_ctx

def sq_relu_mlp(h, w_up, w_down):
    return jnp.square(jax.nn.relu(h @ w_up)) @ w_down

def setup_inputs(seed: int = 0) -> dict:
    key = jax.random.key(seed)
    ks = jax.random.split(key, 21)
    f32 = jnp.float32

    def nrm(k, shape, scale):
        return jax.random.normal(k, shape, f32) * scale

    def gain(k, shape):
        return 1.0 + 0.05 * jax.random.normal(k, shape, f32)

    return {
        'x': nrm(ks[0], (BATCH, SEQ, D_MODEL), 1.0),
        'c': nrm(ks[1], (BATCH, D_MODEL), 1.0),
        'ctx': nrm(ks[2], (BATCH, CTX_LEN, D_MODEL), 1.0),
        'c_ctx': nrm(ks[3], (D_MODEL,), 1.0),
        'w_ada': nrm(ks[4], (DEPTH, D_MODEL, 6 * D_MODEL), 0.5 * D_MODEL ** -0.5),
        'b_ada': nrm(ks[5], (DEPTH, 6 * D_MODEL), 0.02),
        'norm_attn_g': gain(ks[6], (DEPTH, D_MODEL)),
        'w_in': nrm(ks[7], (DEPTH, D_MODEL, IN_COLS), D_MODEL ** -0.5),
        'na_rpb': nrm(ks[8], (DEPTH, HEADS, 2 * NA_WIN_R - 1, 2 * NA_WIN_C - 1), 0.1),
        'mla_q_norm_g': gain(ks[9], (DEPTH, MLA_Q_LORA)),
        'mla_w_uq': nrm(ks[10], (DEPTH, MLA_Q_LORA, HEADS * (MLA_NOPE + MLA_ROPE)), MLA_Q_LORA ** -0.5),
        'mla_kv_norm_g': gain(ks[11], (DEPTH, MLA_KV_LORA)),
        'mla_w_ukv': nrm(ks[12], (DEPTH, MLA_KV_LORA, HEADS * (MLA_NOPE + MLA_V)), MLA_KV_LORA ** -0.5),
        'swa_sink': nrm(ks[13], (DEPTH, HEADS), 0.5),
        'diff_lambda': nrm(ks[14], (DEPTH, 4, DIFF_DH), 0.1),
        'diff_norm_g': gain(ks[15], (DEPTH, HEAD_DIM)),
        'w_out': nrm(ks[16], (DEPTH, MIX_WIDTH, D_MODEL), MIX_WIDTH ** -0.5),
        'norm_mlp_g': gain(ks[17], (DEPTH, D_MODEL)),
        'w_up': nrm(ks[18], (DEPTH, D_MODEL, D_FF), D_MODEL ** -0.5),
        'w_down': nrm(ks[19], (DEPTH, D_FF, D_MODEL), D_FF ** -0.5),
        'final_norm_g': gain(ks[20], (D_MODEL,)),
    }

def reference(x, c, ctx, c_ctx, w_ada, b_ada, norm_attn_g, w_in, na_rpb, mla_q_norm_g, mla_w_uq,
              mla_kv_norm_g, mla_w_ukv, swa_sink, diff_lambda, diff_norm_g, w_out, norm_mlp_g,
              w_up, w_down, final_norm_g):
    S = x.shape[1]
    t = jnp.arange(S)
    row, col = t // GRID_W, t % GRID_W
    rope64 = axial_rope(row, col, HEAD_DIM)
    rope32 = axial_rope(row, col, MLA_ROPE)
    c_act = jax.nn.silu(c)
    cc_act = jax.nn.silu(c_ctx)
    xl, xc = x, ctx
    for l in range(DEPTH):
        need_ctx = l < DEPTH - 1
        lam_init = 0.8 - 0.6 * math.exp(-0.3 * l)
        mod_l = jnp.split((c_act @ w_ada[l] + b_ada[l])[:, None, :], 6, axis=-1)
        mod_c = jnp.split(cc_act @ w_ada[l] + b_ada[l], 6, axis=-1)
        hl = modulate(rmsnorm(xl, norm_attn_g[l]), mod_l[0], mod_l[1])
        hc = modulate(rmsnorm(xc, norm_attn_g[l]), mod_c[0], mod_c[1])
        zl = split_cols(hl @ w_in[l])
        zc = split_cols(hc @ w_in[l])
        oa_l, oa_c = neighbourhood_attention(zl[0:3], zc[0:3], na_rpb[l], need_ctx)
        ob_l, ob_c = latent_attention(zl[3:6], zc[3:6], mla_q_norm_g[l], mla_w_uq[l],
                                      mla_kv_norm_g[l], mla_w_ukv[l], rope32, need_ctx)
        oc_l, oc_c = window_attention(zl[6:9], zc[6:9], swa_sink[l], rope64, need_ctx)
        od_l, od_c = differential_attention(zl[9:12], zc[9:12], diff_lambda[l], diff_norm_g[l],
                                            lam_init, rope32, need_ctx)
        mix_l = jnp.concatenate([oa_l, ob_l, oc_l, od_l], axis=-1)
        xl = xl + mod_l[2] * (mix_l @ w_out[l])
        hl = modulate(rmsnorm(xl, norm_mlp_g[l]), mod_l[3], mod_l[4])
        xl = xl + mod_l[5] * sq_relu_mlp(hl, w_up[l], w_down[l])
        if need_ctx:
            mix_c = jnp.concatenate([oa_c, ob_c, oc_c, od_c], axis=-1)
            xc = xc + mod_c[2] * (mix_c @ w_out[l])
            hc = modulate(rmsnorm(xc, norm_mlp_g[l]), mod_c[3], mod_c[4])
            xc = xc + mod_c[5] * sq_relu_mlp(hc, w_up[l], w_down[l])
    return rmsnorm(xl, final_norm_g)


_drawn_inputs = setup_inputs


def setup_inputs(seed=0):
    import zlib

    import numpy as np

    out = dict(_drawn_inputs(seed))
    spreads = {}
    factors = {'norm_attn_g': 7.021,
     'na_rpb': 8.0,
     'mla_q_norm_g': 8.0,
     'mla_w_uq': 2.81,
     'mla_kv_norm_g': 8.0,
     'swa_sink': 8.0,
     'diff_lambda': 3.496,
     'diff_norm_g': 7.517}
    for name, (base, spread) in spreads.items():
        noise = np.random.default_rng([zlib.crc32(name.encode()), seed]).standard_normal(out[name].shape)
        drawn = base * np.exp(spread * noise) if base else spread * noise
        out[name] = jnp.asarray(drawn.astype(out[name].dtype))
    for name, factor in factors.items():
        out[name] = (out[name] * factor).astype(out[name].dtype)
    return out
```

```python
from contextlib import ExitStack

import numpy as np

import concourse.bass as bass
from concourse import mybir

P = 128
D = 1024
KT = D // P
S, C = 512, 256
TOK = S + C
DEPTH = 2
HEADS, DH = 4, 64
GRID_W = 64
NA_COLS = 16
QLORA, KVLORA, ROPE = 192, 128, 32
NCHUNK = 32
NQ = 4
CPQ = NCHUNK // NQ
NADA = 6 * KT
EPS = 1e-6
NEG = -1e30
LOWEST = -3.0e38
ROPE_BASE = 10000.0
LAM_INIT = [0.8 - 0.6 * float(np.exp(-0.3 * l)) for l in range(DEPTH)]

GROUPS = "ACBD"
TILES = {
    "A": [("q", 0), ("q", 1), ("k", 2), ("k", 3), ("v", 0), ("v", 1)],
    "B": [("cq", 0), ("cqkr", 1), ("ckv", 2)],
    "C": [("qr", 0), ("qr", 1), ("kr", 2), ("v", 0)],
    "D": [("qr", 0), ("qr", 1), ("kr", 2), ("kr", 3), ("v", 0), ("v", 1)],
}
TILE0 = {"A": 0, "B": 6, "C": 9, "D": 13}
NIN = 19
MIX0 = {"A": 0, "B": 2, "C": 4, "D": 6}
SCALE = {"A": DH ** -0.5, "B": (DH + ROPE) ** -0.5, "C": DH ** -0.5, "D": (DH // 2) ** -0.5}

V_BADA, V_GATTN, V_GMLP, V_GQ, V_GKV, V_DNG, V_SINK, V_LAM = 0, 48, 56, 64, 66, 67, 68, 72
V_LEN = 72 + 128
M_ID, M_ONES, M_BONES, M_P64, M_P32, M_REP, M_RROT = range(7)

RAW, WR, ZR, PR = 3, 3, 3, 4
LAG = 2

F32 = mybir.dt.float32
F32R = mybir.dt.float32r
ALU = mybir.AluOpType
ACT = mybir.ActivationFunctionType
AXX = mybir.AxisListType.X


def segs(width):
    return [(0, S)] + ([(S, C)] if width > S else [])


class Step:

    def __init__(self, kind=None, acc=None, b=None, br=None, c=None, col=None, comps=None, done=None, first=None,
                 g=None, gin=None, h=None, hb=None, hi=None, hs=None, i=None, j=None, job=None, jobs=None, kt=None,
                 l=None, last=None, lo=None, loc=None, m=None, mix=None, mul=None, n=None, pieces=None, qlo=None,
                 qp=None, qt=None, relu=None, slot=None, sq=None, std=None, su=None, sum=None, t=None, tiles=None,
                 tr=None, tu=None, u2=None, un=None, units=None, us=None, uses=None, what=None, which=None, width=None,
                 wl=None, wq=None, x=None, z=None, zd=None):
        self.kind = kind
        self.acc = acc
        self.b = b
        self.br = br
        self.c = c
        self.col = col
        self.comps = comps
        self.done = done
        self.first = first
        self.g = g
        self.gin = gin
        self.h = h
        self.hb = hb
        self.hi = hi
        self.hs = hs
        self.i = i
        self.j = j
        self.job = job
        self.jobs = jobs
        self.kt = kt
        self.l = l
        self.last = last
        self.lo = lo
        self.loc = loc
        self.m = m
        self.mix = mix
        self.mul = mul
        self.n = n
        self.pieces = pieces
        self.qlo = qlo
        self.qp = qp
        self.qt = qt
        self.relu = relu
        self.slot = slot
        self.sq = sq
        self.std = std
        self.su = su
        self.sum = sum
        self.t = t
        self.tiles = tiles
        self.tr = tr
        self.tu = tu
        self.u2 = u2
        self.un = un
        self.units = units
        self.us = us
        self.uses = uses
        self.what = what
        self.which = which
        self.width = width
        self.wl = wl
        self.wq = wq
        self.x = x
        self.z = z
        self.zd = zd


class Plan:

    def __init__(self):
        self.n = {}
        self.raw = []
        self.raw_free = []
        self.big_free = []
        self.t_free = []
        self.o_free = []
        self.z_free = [[] for _ in range(ZR)]
        self.nz = 0
        self.steps = []
        self.build()

    def tick(self, name):
        self.n[name] = self.n.get(name, 0) + 1
        return self.n[name]

    def add(self, kind, **kw):
        s = Step(kind=kind, **kw)
        self.steps.append(s)
        return s

    def big(self):
        self.big_free.append(None)
        return len(self.big_free) - 1, self.tick("big_ready")

    def tbank(self):
        self.t_free.append(None)
        return len(self.t_free) - 1, self.tick("t_ready")

    def wblock(self, name, l, idx):
        i = self.tick("split_done")
        self.raw.append((name, l, idx))
        self.raw_free.append(("split_done", i))
        return Step(n=len(self.raw) - 1, i=i)

    def hilo(self):
        return self.tick("hi_done"), self.tick("lo_done")

    def ada(self, l, count):
        for _ in range(count):
            j = self.ada_next[l]
            if j >= NADA:
                return
            self.ada_next[l] += 1
            tu, tr = self.tbank()
            self.raw.append(("ada", l, j))
            self.raw_free.append(("t_ready", tr))
            done = self.tick("ada_done")
            self.t_free[tu] = ("ada_done", done)
            self.ada_at[l, j] = done
            self.add("ada", l=l, j=j, n=len(self.raw) - 1, tu=tu, tr=tr, done=done)

    def ssq(self, m, width):
        a = self.tick("sq_done")
        d = self.tick("acc_done") if m else None
        self.add("ssq", m=m, width=width, sq=a, acc=d)

    def norm(self, l, which, width):
        su, br = self.big()
        std = self.tick("std_done")
        self.big_free[su] = ("std_done", std)
        sq, acc = self.n["sq_done"], self.n["acc_done"]
        hs = []
        for _ in range(KT):
            if which == "final":
                hs.append(self.tick("y_done"))
            else:
                t = self.tick("t_done")
                hs.append((t, *self.hilo()))
        self.h_at = hs
        self.z_free = [[] for _ in range(ZR)]
        self.add("norm", l=l, which=which, width=width, su=su, br=br, std=std, acc=acc, hs=hs)

    def zslot(self):
        z = self.nz % ZR
        self.nz += 1
        w, self.z_free[z] = self.z_free[z], []
        return z, w

    def inproj(self, l, g):
        self.nz = 0
        self.gin += {"A": 0, "C": 2, "B": 3, "D": 0}[g]
        post = []
        for j, (what, slot) in enumerate(TILES[g]):
            width = S if (l == DEPTH - 1 and what in ("q", "qr", "cq")) else TOK
            b = self.wblock("in", l, TILE0[g] + j)
            su, br = self.big()
            b.end = br
            st = self.add("in", l=l, g=g, b=b, su=su, br=br, what=what, slot=slot, width=width, first=(j == 0), hs=self.h_at)
            if what in ("q", "k"):
                st.hi, st.lo = self.hilo()
                self.big_free[su] = ("lo_done", st.lo)
            else:
                st.z, st.zwait = self.zslot()
                st.zd = self.tick("z_done")
                self.big_free[su] = ("z_done", st.zd)
            if l == 0:
                self.ada(0, 2)
            for p in post:
                self.post(*p)
            post = [(l, g, what, slot, width, st)] if what in ("v", "qr", "kr") else []
        for p in post:
            self.post(*p)
        if g == "B":
            self.bprep(l)

    def post(self, l, g, what, slot, width, src):
        if what == "v":
            pieces = []
            for kt, n in ((0, 4), (4, 2)):
                tu, tr = self.tbank()
                hi, lo = self.hilo()
                self.t_free[tu] = ("lo_done", lo)
                pieces.append(Step(kt=kt, n=n, tu=tu, tr=tr, hi=hi, lo=lo))
            self.z_free[src.z] = [("t_ready", pieces[-1].tr)]
            self.add("vpost", slot=slot, z=src.z, zd=src.zd, pieces=pieces)
        else:
            tu, tr = self.tbank()
            mul = self.tick("rope_done")
            rs = self.tick("rope_done")
            hi, lo = self.hilo()
            self.t_free[tu] = ("rope_done", mul)
            self.z_free[src.z] = [("lo_done", lo)]
            self.add("rope", g=g, gin=self.gin, slot=slot, z=src.z, zd=src.zd, width=width, tu=tu, tr=tr, mul=mul, sum=rs, hi=hi, lo=lo)

    def bprep(self, l):
        wq = S if l == DEPTH - 1 else TOK
        s = self.add("bprep", l=l, gin=self.gin, wq=wq, zd=self.n["z_done"])
        s.sq = [self.tick("sq_done") for _ in range(3)]
        s.ssq_q, s.ssq_kv = self.big(), self.big()
        s.std = [self.tick("std_done") for _ in range(2)]
        self.big_free[s.ssq_q[0]] = ("std_done", s.std[0])
        self.big_free[s.ssq_kv[0]] = ("std_done", s.std[1])
        s.cn = [self.tick("cn_done") for _ in range(2)]
        s.rep, s.krot = self.big(), self.tbank()
        s.krope = self.tick("rope_done")
        self.big_free[s.rep[0]] = ("rope_done", s.krope)
        self.t_free[s.krot[0]] = ("rope_done", s.krope)
        s.khl = self.hilo()
        s.q = []
        for _ in range(2):
            u = self.big()
            hl = self.hilo()
            self.big_free[u[0]] = ("lo_done", hl[1])
            s.q.append((u, hl))
        s.qr = self.big()
        s.qz = self.tick("z_done")
        self.big_free[s.qr[0]] = ("z_done", s.qz)
        s.k = []
        for _ in range(2):
            u = self.big()
            hl = self.hilo()
            self.big_free[u[0]] = ("lo_done", hl[1])
            s.k.append((u, hl))
        s.qrot = self.tbank()
        s.qmul = self.tick("rope_done")
        s.qrope = self.tick("rope_done")
        self.t_free[s.qrot[0]] = ("rope_done", s.qmul)
        s.qhl = self.hilo()
        s.v = []
        for _ in range(3):
            u = self.tbank()
            hl = self.hilo()
            self.t_free[u[0]] = ("lo_done", hl[1])
            s.v.append((u, hl))

    def attention(self, l, g):
        units, jobs = [], []
        comps = 2 if g == "D" else 1
        last_qt = 6 if l < DEPTH - 1 else 4
        qlo = self.n["lo_done"]
        for h in range(HEADS):
            for qp in range(last_qt // 2):
                job = Step(h=h, qp=qp, tiles=[])
                for qt in (2 * qp, 2 * qp + 1):
                    if qt >= 4:
                        loc = []
                    elif g == "C":
                        loc = list(range(max(0, qt - 1), min(3, qt + 1) + 1))
                    else:
                        loc = list(range(4))
                    for t in range(comps):
                        u = Step(h=h, qt=qt, t=t, loc=loc, wl=len(loc) * P, job=job, un=self.nu,
                                 pieces=[], last=(t == comps - 1))
                        self.nu += 1
                        u.w = u.wl + C
                        u.biased = g in "AC" and bool(loc)
                        units.append(u)
                        job.tiles.append((qt, loc)) if u.last else None
                jobs.append(job)
        st = self.add("attn", l=l, g=g, gin=self.gin, units=units, jobs=jobs, qlo=qlo, comps=comps)
        for i in range(len(units) + LAG + 1):
            if i < len(units):
                u = units[i]
                u.su, u.br = self.big()
                if u.biased:
                    u.bias = [self.tick("bias_done"), self.tick("bias_done")]
                u.nm = self.tick("nmax_done")
                u.exp = self.tick("exp_done")
                self.big_free[u.su] = ("bias_done", u.bias[1]) if u.biased else ("exp_done", u.exp)
                u.r = self.tick("r_done")
                u.pn = self.tick("pnorm_done") if not (g == "D" and u.t == 1) else None
                u.df = self.tick("diff_done") if g == "D" and u.t == 1 else None
            j = i - LAG - 1
            if 0 <= j < len(units) and units[j].last and units[j].job.tiles[-1][0] == units[j].qt:
                job = units[j].job
                self.o_free.append(None)
                job.ou = len(self.o_free) - 1
                job.ready = self.tick("o_ready")
                job.half = self.tick("half_done")
                job.sum = self.tick("osum_done")
                self.o_free[job.ou] = job.sum
            j = i - LAG
            if 0 <= j < len(units) and units[j].last:
                u = units[j]
                parts = ([(u.loc[0], len(u.loc), 0)] if u.loc else []) + [(4, 2, u.wl)]
                for kt, n, col in parts:
                    tu, tr = self.tbank()
                    hi, lo = self.hilo()
                    self.t_free[tu] = ("lo_done", lo)
                    u.pieces.append(Step(kt=kt, n=n, col=col, tu=tu, tr=tr, hi=hi, lo=lo))
        st.end_o = self.n["o_ready"]
        st.end_sum = self.n["osum_done"]
        if g == "D":
            st.dn = []
            for t in range(2):
                d = Step(sq=self.tick("sq_done"))
                d.su, d.br = self.big()
                d.std = self.tick("std_done")
                self.big_free[d.su] = ("std_done", d.std)
                d.done = self.tick("cn_done")
                st.dn.append(d)
        st.mix = [self.tick("mix_done") for _ in range(2)]
        st.prev_out = self.last_out
        for z in range(ZR):
            self.z_free[z] = [("mix_done", st.mix[1])]

    def mlp(self, l):
        width = TOK if l < DEPTH - 1 else S
        for qd in range(NQ):
            us = []
            for c in range(CPQ):
                b = self.wblock("up", l, qd * CPQ + c)
                su, br = self.big()
                relu = self.tick("relu_done")
                self.big_free[su] = ("relu_done", relu)
                u2 = self.tick("u2_done")
                hi, lo = self.hilo()
                us.append(lo)
                b.end = br
                self.add("up", l=l, b=b, c=c, su=su, br=br, relu=relu, u2=u2, hi=hi, lo=lo, width=width, hs=self.h_at)
                if l + 1 < DEPTH:
                    self.ada(l + 1, 1)
            for m in range(KT):
                b = self.wblock("down", l, qd * KT + m)
                su, br = self.big()
                x = self.tick("x_done")
                self.big_free[su] = ("x_done", x)
                b.end = br
                self.add("down", l=l, b=b, m=m, su=su, br=br, x=x, us=us, width=width)
                if qd == NQ - 1:
                    self.ssq(m, width)
                    self.steps[-1].after = x
                if l + 1 < DEPTH:
                    self.ada(l + 1, 1)

    def build(self):
        self.nu = 0
        self.gin = 0
        self.ada_next = [0] * DEPTH
        self.ada_at = {}
        self.last_out = None
        for m in range(KT):
            self.ssq(m, TOK)
            self.steps[-1].after = None
        self.ada(0, 2 * KT)
        for l in range(DEPTH):
            self.norm(l, "attn", TOK)
            for g in GROUPS:
                self.inproj(l, g)
                self.attention(l, g)
                self.outproj(l, g)
            self.norm(l, "mlp", TOK if l < DEPTH - 1 else S)
            self.mlp(l)
        self.norm(DEPTH - 1, "final", S)
        blocks = [s.b for s in self.steps if s.kind in ("in", "out", "up", "down")]
        users = [s for s in self.steps if s.kind in ("in", "out", "up", "down")]
        for i, s in enumerate(users):
            s.ahead = blocks[0:3] if i == 0 else blocks[i + 2:i + 3]
            for b in s.ahead:
                b.before = blocks[b.i - 1 - WR].end if b.i > WR else 0

    def outproj(self, l, g):
        st = self.steps[-1]
        width = TOK if l < DEPTH - 1 else S
        for hb in range(2):
            b = self.wblock("out", l, MIX0[g] + hb)
            uses = []
            for mm in range(4):
                su, br = self.big()
                x = self.tick("x_done")
                self.big_free[su] = ("x_done", x)
                uses.append(Step(m=4 * hb + mm, su=su, br=br, x=x))
            b.end = uses[-1].br
            st.out_n = b.n
            self.add("out", l=l, g=g, b=b, hb=hb, uses=uses, width=width, mix=st.mix[1])
            if g == GROUPS[-1]:
                for u in uses:
                    self.ssq(u.m, width)
                    self.steps[-1].after = u.x
            self.last_out = uses[-1].br


def build_program(nc, xt, cvec, vecs, gfin, mats, rope, maskna, masksw, rpb, wuq, wukv,
                  w_ada, w_in, w_out, w_up, w_down, out):
    plan = Plan()
    dram = {"ada": w_ada, "in": w_in, "out": w_out, "up": w_up, "down": w_down}
    steps = plan.steps

    with ExitStack() as ctx:
        def sb(name, shape, dt=F32):
            return ctx.enter_context(nc.sbuf_tensor(name, shape, dt))

        x = sb("x", [P, KT, TOK])
        h_hi, h_lo = sb("h_hi", [P, KT, TOK], F32R), sb("h_lo", [P, KT, TOK], F32R)
        arena = sb("arena", [P, 16, TOK], F32R)
        pt = sb("pt", [P, 2, 6, 2 * P], F32R)
        raw = sb("raw", [P, RAW, D])
        w_hi, w_lo = sb("w_hi", [P, WR, D], F32R), sb("w_lo", [P, WR, D], F32R)
        z = sb("z", [P, ZR, TOK])
        gs = sb("gs", [P, 2048])
        pb = sb("pb", [P, PR, TOK])
        mix_hi, mix_lo = sb("mix_hi", [P, 2, TOK], F32R), sb("mix_lo", [P, 2, TOK], F32R)
        rt = sb("rt", [P, 2, S])
        mt = sb("mt", [P, 7, P])
        mna = sb("mna", [P, GRID_W])
        zeros = sb("zeros", [P, C])
        vec = sb("vec", [P, DEPTH, V_LEN])
        gf = sb("gf", [P, KT])
        cv, cs = sb("cv", [P, KT, 2]), sb("cs", [P, KT, 2])
        ada = sb("ada", [P, DEPTH, NADA, 2])
        amul = sb("amul", [P, KT, 2])
        otmp = sb("otmp", [DH, 2, 2 * P])
        col = sb("col", [P, 8, 8])
        eps = sb("eps", [P, 1])
        lam = sb("lam", [P, 8])
        nsink = sb("nsink", [P, HEADS])
        dgain = sb("dgain", [P, 1])
        MX, MX2, NM, L, ES, R, RL = range(7)

        big = [ctx.enter_context(nc.psum_tensor(f"big{i}", [P, 1024], F32)) for i in range(2)]
        tb = [ctx.enter_context(nc.psum_tensor(f"tb{i}", [P, 512], F32)) for i in range(2)]
        ob = [ctx.enter_context(nc.psum_tensor(f"ob{i}", [P, 512], F32)) for i in range(2)]

        def semaphore(name):
            return ctx.enter_context(nc.semaphore(name))

        acc_done = semaphore("acc_done")
        ada_done = semaphore("ada_done")
        bias_done = semaphore("bias_done")
        big_ready = semaphore("big_ready")
        cexp_done = semaphore("cexp_done")
        cn_done = semaphore("cn_done")
        const_in = semaphore("const_in")
        diff_done = semaphore("diff_done")
        dve_step = semaphore("dve_step")
        exp_done = semaphore("exp_done")
        group_in = semaphore("group_in")
        half_done = semaphore("half_done")
        hi_done = semaphore("hi_done")
        hi_split = semaphore("hi_split")
        lam_dot = semaphore("lam_dot")
        lam_exp = semaphore("lam_exp")
        ln_done = semaphore("ln_done")
        lo_done = semaphore("lo_done")
        mix_done = semaphore("mix_done")
        mix_half = semaphore("mix_half")
        nmax_done = semaphore("nmax_done")
        o_ready = semaphore("o_ready")
        osum_done = semaphore("osum_done")
        pnorm_done = semaphore("pnorm_done")
        r_done = semaphore("r_done")
        relu_done = semaphore("relu_done")
        rope_done = semaphore("rope_done")
        silu_done = semaphore("silu_done")
        split_done = semaphore("split_done")
        sq_done = semaphore("sq_done")
        std_done = semaphore("std_done")
        t_done = semaphore("t_done")
        t_ready = semaphore("t_ready")
        u2_done = semaphore("u2_done")
        x_done = semaphore("x_done")
        x_in = semaphore("x_in")
        y_done = semaphore("y_done")
        z_done = semaphore("z_done")
        zeros_done = semaphore("zeros_done")
        raw_in = [semaphore(f"raw_in{i}") for i in range(RAW)]
        bias_in = [semaphore(f"bias_in{i}") for i in range(2)]
        out_done = [semaphore(f"out_done{i}") for i in range(PR)]
        sems = {"split_done": split_done, "t_ready": t_ready, "lo_done": lo_done, "z_done": z_done, "exp_done": exp_done,
                "bias_done": bias_done, "x_done": x_done, "relu_done": relu_done, "std_done": std_done,
                "rope_done": rope_done, "ada_done": ada_done, "mix_done": mix_done}
        block = ctx.enter_context(nc.Block())

        def big_free(use):
            name, value = plan.big_free[use - 2]
            return sems[name], value

        def t_free(use):
            name, value = plan.t_free[use - 2]
            return sems[name], value

        def qk(slot, part):
            return arena[:, 2 * slot + part, :]

        vals = arena[:, 12:16, :].rearrange("p a b -> p (a b)").rearrange(
            "p (t h s d) -> p t h s d", t=6, h=HEADS, s=2)

        def as32(ap):
            return ap.bitcast(F32)

        attns = [s for s in steps if s.kind == "attn"]
        group_no = {}
        for k, s in enumerate(attns):
            group_no[s.l, s.g] = k

        @block.sync
        def _(sp):
            sp.dma_start(x[:, :, :], xt).then_inc(x_in, 16)
            for dst, src in ((vec[:, :, :], vecs), (gf[:, :], gfin), (cv[:, :, :], cvec),
                             (mt[:, :, :], mats), (mna[:, :], maskna)):
                sp.dma_start(dst, src).then_inc(const_in, 16)
            at = 0

            def blocks_until(n):
                nonlocal at
                while at < n:
                    name, l, idx = plan.raw[at]
                    if at >= RAW:
                        freed_by, value = plan.raw_free[at - RAW]
                        sp.wait_ge(sems[freed_by], value)
                    sp.dma_start(raw[:, at % RAW, :], dram[name][l, idx]).then_inc(raw_in[at % RAW], 16)
                    at += 1

            for s in steps:
                if s.kind == "in":
                    blocks_until(s.b.n + 1)
                    if s.first:
                        k = group_no[s.l, s.g]
                        if k:
                            sp.wait_ge(mix_done, attns[k - 1].mix[1])
                        if s.g == "A":
                            for h in range(2):
                                sp.dma_start(gs[:, h * 1024:(h + 1) * 1024], rpb[s.l, h]).then_inc(bias_in[h], 16)
                        if s.g == "C":
                            sp.dma_start(rt[:, :, :], rope[0]).then_inc(group_in, 16)
                            sp.dma_start(gs[:, 0:3 * P], masksw).then_inc(group_in, 16)
                        if s.g == "B":
                            sp.dma_start(rt[:, :, :], rope[1]).then_inc(group_in, 16)
                            sp.dma_start(gs[:, 0:768], wuq[s.l]).then_inc(group_in, 16)
                            sp.dma_start(gs[:, 768:1280], wukv[s.l]).then_inc(group_in, 16)
                if s.kind == "attn":
                    blocks_until(s.out_n + 1)
                if s.kind == "attn" and s.g == "A":
                    for h in range(2, HEADS):
                        sp.wait_ge(bias_done, max(u.bias[1] for u in s.units if u.h == h - 2 and u.biased))
                        sp.dma_start(gs[:, (h - 2) * 1024:(h - 1) * 1024], rpb[s.l, h]).then_inc(bias_in[h - 2], 16)
                if s.kind in ("ada",):
                    blocks_until(s.n + 1)
                if s.kind in ("out", "up", "down"):
                    blocks_until(s.b.n + 1)
                if s.kind == "norm" and s.which == "final":
                    for k in range(KT):
                        sp.wait_ge(y_done, s.hs[k])
                        sp.dma_start(out[:, k, :], pb[:, k % PR, 0:S]).then_inc(out_done[k % PR], 16)
            for k in range(PR):
                sp.wait_ge(out_done[k], 16 * (KT // PR))

        @block.gpsimd
        def _(pool):
            def split_lo(b):
                pool.wait_ge(hi_split, b.i)
                sl = (b.i - 1) % WR
                pool.tensor_tensor(w_lo[:, sl, :], raw[:, b.n % RAW, :], as32(w_hi[:, sl, :]), ALU.subtract).then_inc(split_done, 1)

            for s in steps:
                if s.kind in ("in", "out", "up", "down"):
                    for b in s.ahead:
                        split_lo(b)
                if s.kind == "attn":
                    width = TOK if s.l < DEPTH - 1 else S
                    if s.prev_out:
                        pool.wait_ge(big_ready, s.prev_out)
                    for t in range(2):
                        if s.g == "D":
                            pool.wait_ge(cn_done, s.dn[t].done)
                        else:
                            pool.wait_ge(osum_done, max(j.sum for j in s.jobs if j.h // 2 == t))
                        zz = z[:, t, 0:width]
                        pool.tensor_copy(mix_hi[:, t, 0:width], zz).then_inc(mix_half, 1)
                        pool.wait_ge(mix_half, s.mix[t])
                        pool.tensor_tensor(mix_lo[:, t, 0:width], zz, as32(mix_hi[:, t, 0:width]), ALU.subtract).then_inc(mix_done, 1)

        @block.scalar
        def _(act):
            def hi_copy(dst, src, value):
                act.activation(dst, src, ACT.Copy).then_inc(hi_done, 1)

            def rope_hi(s_hi, s_sum, src, slot, width):
                act.wait_ge(rope_done, s_sum)
                hi_copy(qk(slot, 0)[:, 0:width], src, s_hi)

            def rsqrt(dst, tmp, total, n, value):
                act.activation(tmp, total, ACT.Ln, bias=eps[:, :], scale=1.0 / n).then_inc(ln_done, 1)
                act.wait_ge(ln_done, value)
                act.activation(dst, tmp, ACT.Exp, scale=-0.5).then_inc(std_done, 1)

            def split_hi(b):
                act.wait_ge(raw_in[b.n % RAW], 16 * (b.n // RAW + 1))
                if b.before:
                    act.wait_ge(big_ready, b.before)
                act.activation(w_hi[:, (b.i - 1) % WR, :], raw[:, b.n % RAW, :], ACT.Copy).then_inc(hi_split, 1)

            act.wait_ge(const_in, 16 * 5)
            act.activation(amul[:, :, :], cv[:, :, :], ACT.Exp, scale=-1.0).then_inc(cexp_done, 1)
            act.wait_ge(x_in, 16)
            act.wait_ge(zeros_done, 2)
            for s in steps:
                if s.kind in ("in", "out", "up", "down"):
                    for b in s.ahead:
                        split_hi(b)
                if s.kind == "ssq":
                    if s.after:
                        act.wait_ge(x_done, s.after)
                    if s.m >= 3:
                        act.wait_ge(acc_done, s.acc - 2)
                    dst = z[:, 2 if s.m == 0 else s.m % 2, 0:s.width]
                    act.activation(dst, x[:, s.m, 0:s.width], ACT.Square).then_inc(sq_done, 1)
                elif s.kind == "norm":
                    act.wait_ge(big_ready, s.br)
                    rsqrt(z[:, 1, 0:s.width], z[:, 0, 0:s.width], big[s.su % 2][:, 0:s.width], D, s.std)
                    if s.which == "final":
                        continue
                    shift = 0 if s.which == "attn" else 3 * KT
                    for k in range(KT):
                        act.wait_ge(t_done, s.hs[k][0])
                        for v, (c0, n) in enumerate(segs(s.width)):
                            ins = act.activation(h_hi[:, k, c0:c0 + n], pb[:, k % PR, c0:c0 + n], ACT.Identity,
                                                 bias=ada[:, s.l, shift + k, v:v + 1])
                        ins.then_inc(hi_done, 1)
                elif s.kind == "in":
                    act.wait_ge(big_ready, s.br)
                    src = big[s.su % 2][:, 0:s.width]
                    if s.what in ("q", "k"):
                        hi_copy(qk(s.slot, 0)[:, 0:s.width], src, s.hi)
                    else:
                        for name, value in s.zwait:
                            act.wait_ge(sems[name], value)
                        act.activation(z[:, s.z, 0:s.width], src, ACT.Copy).then_inc(z_done, 1)
                elif s.kind == "vpost":
                    for p in s.pieces:
                        act.wait_ge(t_ready, p.tr)
                        src = tb[p.tu % 2][:, 0:p.n * P].rearrange("p (t h d) -> p t h d", t=p.n, h=2)
                        hi_copy(vals[:, p.kt:p.kt + p.n, 2 * s.slot:2 * s.slot + 2, 0, :], src, p.hi)
                elif s.kind == "rope":
                    rope_hi(s.hi, s.sum, z[:, s.z, 0:s.width], s.slot, s.width)
                elif s.kind == "bprep":
                    act.wait_ge(z_done, s.zd)
                    act.activation(pb[:, 0, 0:s.wq], z[:, 0, 0:s.wq], ACT.Square).then_inc(sq_done, 1)
                    act.activation(pb[0:DH, 1, 0:s.wq], z[0:DH, 1, 0:s.wq], ACT.Square).then_inc(sq_done, 1)
                    act.activation(pb[:, 2, :], z[:, 2, :], ACT.Square).then_inc(sq_done, 1)
                    act.wait_ge(big_ready, s.ssq_q[1])
                    rsqrt(pb[:, 3, 0:s.wq], pb[:, 3, 0:s.wq], big[s.ssq_q[0] % 2][:, 0:s.wq], QLORA, s.std[0])
                    act.wait_ge(big_ready, s.ssq_kv[1])
                    rsqrt(pb[:, 0, :], pb[:, 0, :], big[s.ssq_kv[0] % 2][:, 0:TOK], KVLORA, s.std[1])
                    rope_hi(s.khl[0], s.krope, pb[:, 1, :], 5, TOK)
                    for t, (u, hl) in enumerate(s.q):
                        act.wait_ge(big_ready, u[1])
                        hi_copy(qk(t, 0)[:, 0:s.wq], big[u[0] % 2][:, 0:s.wq], hl[0])
                    act.wait_ge(big_ready, s.qr[1])
                    act.wait_ge(cn_done, s.cn[1])
                    act.activation(pb[:, 3, 0:s.wq], big[s.qr[0] % 2][:, 0:s.wq], ACT.Copy).then_inc(z_done, 1)
                    for t, (u, hl) in enumerate(s.k):
                        act.wait_ge(big_ready, u[1])
                        hi_copy(qk(3 + t, 0), big[u[0] % 2][:, 0:TOK], hl[0])
                    rope_hi(s.qhl[0], s.qrope, pb[:, 3, 0:s.wq], 2, s.wq)
                    for t, (u, hl) in enumerate(s.v):
                        act.wait_ge(t_ready, u[1])
                        hi_copy(vals[:, 2 * t:2 * t + 2, :, 0, :],
                                tb[u[0] % 2][:, :].rearrange("p (t h d) -> p t h d", t=2, h=HEADS), hl[0])
                elif s.kind == "attn":
                    sc = SCALE[s.g]
                    if s.g == "D":
                        act.wait_ge(lam_dot, 2 * s.l + 2)
                        act.activation(lam[:, 2:4], lam[:, 0:2], ACT.Exp).then_inc(lam_exp, 1)
                    for i in range(len(s.units) + LAG + 1):
                        if i < len(s.units):
                            u = s.units[i]
                            c = col[:, u.un % 8, :]
                            pr = pb[:, u.un % PR, 0:u.w]
                            act.wait_ge(nmax_done, u.nm)
                            if i >= PR:
                                v = s.units[i - PR]
                                act.wait_ge(t_ready, (v if v.last else s.units[i - PR + 1]).pieces[-1].tr)
                            src = pr if u.biased else big[u.su % 2][:, S - u.wl:S + C]
                            ins = act.activation(pr, src, ACT.Exp, bias=c[:, NM:NM + 1], scale=sc, accum_out=c[:, L:L + 1])
                            if s.g == "C":
                                ins = act.activation(c[:, ES:ES + 1], vec[:, s.l, V_SINK + u.h:V_SINK + u.h + 1], ACT.Exp,
                                                     bias=c[:, NM:NM + 1])
                            ins.then_inc(exp_done, 1)
                        j = i - LAG - 1
                        if 0 <= j < len(s.units) and s.units[j].job.tiles[-1][0] == s.units[j].qt and s.units[j].last:
                            job = s.units[j].job
                            act.wait_ge(o_ready, job.ready)
                            if job.ou >= 2:
                                act.wait_ge(osum_done, plan.o_free[job.ou - 2])
                            act.activation(otmp[:, job.ou % 2, :], ob[job.ou % 2][DH:P, 0:2 * P], ACT.Copy).then_inc(half_done, 1)
                        j = i - LAG
                        if 0 <= j < len(s.units) and s.units[j].last:
                            u = s.units[j]
                            qc = (u.qt % 2) * P
                            k0 = s.jobs.index(u.job)
                            if k0:
                                act.wait_ge(o_ready, s.jobs[k0 - 1].ready)
                            for p in u.pieces:
                                act.wait_ge(t_ready, p.tr)
                                hi_copy(pt[:, 0, p.kt:p.kt + p.n, qc:qc + P],
                                        tb[p.tu % 2][:, 0:p.n * P].rearrange("p (t q) -> p t q", t=p.n), p.hi)
                    if s.g == "D":
                        width = TOK if s.l < DEPTH - 1 else S
                        act.wait_ge(osum_done, s.end_sum)
                        for t, d in enumerate(s.dn):
                            act.activation(pb[:, t, 0:width], z[:, t, 0:width], ACT.Square).then_inc(sq_done, 1)
                        for t, d in enumerate(s.dn):
                            act.wait_ge(big_ready, d.br)
                            rsqrt(pb[:, t, 0:width], pb[:, t, 0:width], big[d.su % 2][:, 0:width], DH, d.std)
                elif s.kind == "up":
                    act.wait_ge(big_ready, s.br)
                    pa = pb[:, 2 * (s.c % 2), 0:s.width]
                    act.wait_ge(lo_done, s.lo - 2)
                    act.activation(pa, big[s.su % 2][:, 0:s.width], ACT.Relu).then_inc(relu_done, 1)
                    act.wait_ge(relu_done, s.relu)
                    act.activation(arena[:, s.c, 0:s.width], pa, ACT.Square).then_inc(hi_done, 1)

        @block.vector
        def _(dve):
            steps_done = [0]

            def link(ins):
                steps_done[0] += 1
                ins.then_inc(dve_step, 1)
                dve.wait_ge(dve_step, steps_done[0])

            def lo_sub(dst, src, hi, value, hi_value):
                dve.wait_ge(hi_done, hi_value)
                dve.tensor_tensor(dst, src, as32(hi), ALU.subtract).then_inc(lo_done, 1)

            def low(s, k):
                shift = 0 if s.which == "attn" else 3 * KT
                dve.wait_ge(hi_done, s.hs[k][1])
                for v, (c0, n) in enumerate(segs(s.width)):
                    ins = dve.scalar_tensor_tensor(out=h_lo[:, k, c0:c0 + n], in0=pb[:, k % PR, c0:c0 + n],
                                                   scalar=ada[:, s.l, shift + k, v:v + 1],
                                                   in1=as32(h_hi[:, k, c0:c0 + n]), op0=ALU.add, op1=ALU.subtract)
                ins.then_inc(lo_done, 1)

            link(dve.memset(eps[:, :], EPS))
            dve.memset(zeros[:, :], 0.0).then_inc(zeros_done, 1)
            dve.memset(col[:, :, :], 0.0).then_inc(zeros_done, 1)
            dve.wait_ge(zeros_done, 2)
            dve.wait_ge(cexp_done, 1)
            dve.wait_ge(const_in, 16 * 5)
            link(dve.tensor_scalar(amul[:, :, :], amul[:, :, :], 1.0, None, ALU.add))
            link(dve.reciprocal(amul[:, :, :], amul[:, :, :]))
            dve.tensor_tensor(cs[:, :, :], cv[:, :, :], amul[:, :, :], ALU.mult).then_inc(silu_done, 1)
            n_bias = [0, 0]
            for s in steps:
                if s.kind == "ssq":
                    dve.wait_ge(sq_done, s.sq)
                    if s.m:
                        if s.m > 1:
                            dve.wait_ge(acc_done, s.acc - 1)
                        dve.tensor_tensor(z[:, 2, 0:s.width], z[:, 2, 0:s.width], z[:, s.m % 2, 0:s.width], ALU.add).then_inc(acc_done, 1)
                elif s.kind == "ada":
                    dve.wait_ge(t_ready, s.tr)
                    dve.tensor_scalar(ada[:, s.l, s.j, :], tb[s.tu % 2][:, 0:2], vec[:, s.l, V_BADA + s.j:V_BADA + s.j + 1],
                                           None, ALU.add).then_inc(ada_done, 1)
                elif s.kind == "norm":
                    dve.wait_ge(std_done, s.std)
                    if s.which != "final":
                        base = 0 if s.which == "attn" else 3 * KT
                        gcol = V_GATTN if s.which == "attn" else V_GMLP
                        dve.wait_ge(ada_done, plan.ada_at[s.l, base + 2 * KT - 1])
                        link(dve.scalar_tensor_tensor(out=amul[:, :, :], in0=ada[:, s.l, base + KT:base + 2 * KT, :], scalar=1.0,
                                                      in1=vec[:, s.l, gcol:gcol + KT].unsqueeze(2).broadcast_to([P, KT, 2]),
                                                      op0=ALU.add, op1=ALU.mult))
                    for k in range(KT):
                        if s.which == "final":
                            if k >= PR:
                                dve.wait_ge(out_done[k % PR], 16)
                            dve.scalar_tensor_tensor(out=pb[:, k % PR, 0:S], in0=x[:, k, 0:S], scalar=gf[:, k:k + 1],
                                                          in1=z[:, 1, 0:S], op0=ALU.mult, op1=ALU.mult).then_inc(y_done, 1)
                            continue
                        t, hi, lo = s.hs[k]
                        if k >= PR:
                            dve.wait_ge(lo_done, s.hs[k - PR][2])
                        for v, (c0, n) in enumerate(segs(s.width)):
                            ins = dve.scalar_tensor_tensor(out=pb[:, k % PR, c0:c0 + n], in0=x[:, k, c0:c0 + n],
                                                           scalar=amul[:, k, v:v + 1], in1=z[:, 1, c0:c0 + n],
                                                           op0=ALU.mult, op1=ALU.mult)
                        ins.then_inc(t_done, 1)
                        if k:
                            low(s, k - 1)
                    if s.which != "final":
                        low(s, KT - 1)
                elif s.kind == "in":
                    if s.what in ("q", "k"):
                        dve.wait_ge(big_ready, s.br)
                        lo_sub(qk(s.slot, 1)[:, 0:s.width], big[s.su % 2][:, 0:s.width], qk(s.slot, 0)[:, 0:s.width], s.lo, s.hi)
                elif s.kind == "vpost":
                    for p in s.pieces:
                        dve.wait_ge(t_ready, p.tr)
                        src = tb[p.tu % 2][:, 0:p.n * P].rearrange("p (t h d) -> p t h d", t=p.n, h=2)
                        v = vals[:, p.kt:p.kt + p.n, 2 * s.slot:2 * s.slot + 2]
                        lo_sub(v[:, :, :, 1, :], src, v[:, :, :, 0, :], p.lo, p.hi)
                elif s.kind == "rope":
                    zt = z[:, s.z, :]
                    dve.wait_ge(z_done, s.zd)
                    dve.wait_ge(group_in, 16 * s.gin)
                    dve_tmp = pb[:, 0, 0:S], pb[:, 1, 0:S]
                    dve.wait_ge(lo_done, s.lo - 1)
                    dve.tensor_tensor(dve_tmp[0], zt[:, 0:S], rt[:, 0, :], ALU.mult)
                    dve.wait_ge(t_ready, s.tr)
                    ins = dve.tensor_tensor(dve_tmp[1], tb[s.tu % 2][:, 0:S], rt[:, 1, :], ALU.mult)
                    ins.then_inc(rope_done, 1)
                    dve.wait_ge(rope_done, s.mul)
                    dve.tensor_tensor(zt[:, 0:S], dve_tmp[0], dve_tmp[1], ALU.add).then_inc(rope_done, 1)
                    dve.wait_ge(rope_done, s.sum)
                    lo_sub(qk(s.slot, 1)[:, 0:s.width], zt[:, 0:s.width], qk(s.slot, 0)[:, 0:s.width], s.lo, s.hi)
                elif s.kind == "bprep":
                    dve.wait_ge(group_in, 16 * s.gin)
                    dve.wait_ge(std_done, s.std[0])
                    dve.scalar_tensor_tensor(out=z[:, 0, 0:s.wq], in0=z[:, 0, 0:s.wq], scalar=vec[:, s.l, V_GQ:V_GQ + 1],
                                             in1=pb[:, 3, 0:s.wq], op0=ALU.mult, op1=ALU.mult)
                    dve.scalar_tensor_tensor(out=z[0:DH, 1, 0:s.wq], in0=z[0:DH, 1, 0:s.wq],
                                                  scalar=vec[0:DH, s.l, V_GQ + 1:V_GQ + 2], in1=pb[0:DH, 3, 0:s.wq],
                                                  op0=ALU.mult, op1=ALU.mult).then_inc(cn_done, 1)
                    dve.wait_ge(std_done, s.std[1])
                    dve.scalar_tensor_tensor(out=z[:, 2, :], in0=z[:, 2, :], scalar=vec[:, s.l, V_GKV:V_GKV + 1],
                                                  in1=pb[:, 0, :], op0=ALU.mult, op1=ALU.mult).then_inc(cn_done, 1)
                    dve.wait_ge(big_ready, s.rep[1])
                    dve.wait_ge(t_ready, s.krot[1])
                    rep = big[s.rep[0] % 2]
                    dve.tensor_tensor(pb[:, 1, 0:S], rep[:, 0:S], rt[:, 0, :], ALU.mult)
                    link(dve.tensor_tensor(pb[:, 2, 0:S], tb[s.krot[0] % 2][:, 0:S], rt[:, 1, :], ALU.mult))
                    dve.tensor_tensor(pb[:, 1, 0:S], pb[:, 1, 0:S], pb[:, 2, 0:S], ALU.add)
                    dve.tensor_copy(pb[:, 1, S:TOK], rep[:, S:TOK]).then_inc(rope_done, 1)
                    dve.wait_ge(rope_done, s.krope)
                    lo_sub(qk(5, 1), pb[:, 1, :], qk(5, 0), s.khl[1], s.khl[0])
                    for t, (u, hl) in enumerate(s.q):
                        dve.wait_ge(big_ready, u[1])
                        lo_sub(qk(t, 1)[:, 0:s.wq], big[u[0] % 2][:, 0:s.wq], qk(t, 0)[:, 0:s.wq], hl[1], hl[0])
                    for t, (u, hl) in enumerate(s.k):
                        dve.wait_ge(big_ready, u[1])
                        lo_sub(qk(3 + t, 1), big[u[0] % 2][:, 0:TOK], qk(3 + t, 0), hl[1], hl[0])
                    dve.wait_ge(z_done, s.qz)
                    dve.wait_ge(t_ready, s.qrot[1])
                    dve.tensor_tensor(pb[:, 0, 0:S], pb[:, 3, 0:S], rt[:, 0, :], ALU.mult)
                    dve.tensor_tensor(pb[:, 2, 0:S], tb[s.qrot[0] % 2][:, 0:S], rt[:, 1, :], ALU.mult).then_inc(rope_done, 1)
                    dve.wait_ge(rope_done, s.qmul)
                    dve.tensor_tensor(pb[:, 3, 0:S], pb[:, 0, 0:S], pb[:, 2, 0:S], ALU.add).then_inc(rope_done, 1)
                    dve.wait_ge(rope_done, s.qrope)
                    lo_sub(qk(2, 1)[:, 0:s.wq], pb[:, 3, 0:s.wq], qk(2, 0)[:, 0:s.wq], s.qhl[1], s.qhl[0])
                    for t, (u, hl) in enumerate(s.v):
                        dve.wait_ge(t_ready, u[1])
                        v = vals[:, 2 * t:2 * t + 2]
                        lo_sub(v[:, :, :, 1, :], tb[u[0] % 2][:, :].rearrange("p (t h d) -> p t h d", t=2, h=HEADS),
                               v[:, :, :, 0, :], hl[1], hl[0])
                elif s.kind == "attn":
                    sc = SCALE[s.g]
                    if s.g == "C":
                        link(dve.tensor_scalar(nsink[:, :], vec[:, s.l, V_SINK:V_SINK + HEADS], -1.0, None, ALU.mult))
                    if s.g == "D":
                        for t in range(2):
                            v = vec[:, s.l, V_LAM + 64 * t:V_LAM + 64 * t + 64]
                            dve.tensor_tensor_reduce(pb[:, t, 0:32], v[:, 0:32], v[:, 32:64], 1.0, 0.0, ALU.mult, ALU.add,
                                                     lam[:, t:t + 1]).then_inc(lam_dot, 1)
                        dve.wait_ge(lam_exp, s.l + 1)
                        link(dve.tensor_tensor(lam[:, 4:5], lam[:, 3:4], lam[:, 2:3], ALU.subtract))
                        link(dve.tensor_scalar(lam[:, 5:6], lam[:, 4:5], -LAM_INIT[s.l], None, ALU.add))
                        link(dve.tensor_scalar(dgain[:, :], vec[:, s.l, V_DNG:V_DNG + 1], 1.0 - LAM_INIT[s.l], None, ALU.mult))
                    for i in range(len(s.units) + LAG + 1):
                        if i < len(s.units):
                            u = s.units[i]
                            c = col[:, u.un % 8, :]
                            if u.biased:
                                if s.g == "A":
                                    if u.qt == 0:
                                        b = u.h % 2
                                        n_bias[b] += 1
                                        dve.wait_ge(bias_in[b], 16 * n_bias[b])
                                        tab = gs[:, b * 1024:(b + 1) * 1024].rearrange("p (e c) -> p e c", c=GRID_W)
                                        link(dve.scalar_tensor_tensor(
                                            out=tab, in0=tab, scalar=1.0 / sc,
                                            in1=mna[:, :].unsqueeze(1).broadcast_to([P, 1024 // GRID_W, GRID_W]),
                                            op0=ALU.mult, op1=ALU.add))
                                    off = (u.h % 2) * 1024 + (7 - 2 * u.qt) * GRID_W
                                    bias = gs[:, off:off + S]
                                else:
                                    off = P if u.qt == 0 else 0
                                    bias = gs[:, off:off + u.wl]
                                if i >= PR:
                                    dve.wait_ge(t_ready, s.units[i - PR].pieces[-1].tr)
                                dve.wait_ge(big_ready, u.br)
                                pr = pb[:, u.un % PR, :]
                                sl = big[u.su % 2]
                                dve.tensor_tensor_reduce(pr[:, 0:u.wl], sl[:, S - u.wl:S], bias, 1.0, LOWEST, ALU.add, ALU.max,
                                                              c[:, MX2:MX2 + 1]).then_inc(bias_done, 1)
                                dve.wait_ge(bias_done, u.bias[0])
                                dve.tensor_tensor_reduce(pr[:, u.wl:u.w], sl[:, S:S + C], zeros[:, :], 1.0, c[:, MX2:MX2 + 1],
                                                              ALU.add, ALU.max, c[:, MX:MX + 1]).then_inc(bias_done, 1)
                                dve.wait_ge(bias_done, u.bias[1])
                            else:
                                dve.wait_ge(big_ready, u.br)
                                link(dve.reduce_max(c[:, MX:MX + 1], big[u.su % 2][:, S - u.wl:S + C], AXX))
                            if s.g == "C":
                                ins = dve.tensor_scalar(c[:, NM:NM + 1], c[:, MX:MX + 1], -sc, nsink[:, u.h:u.h + 1],
                                                        ALU.mult, ALU.min)
                            else:
                                ins = dve.tensor_scalar(c[:, NM:NM + 1], c[:, MX:MX + 1], -sc, None, ALU.mult)
                            ins.then_inc(nmax_done, 1)
                        j = i - 1
                        if 0 <= j < len(s.units):
                            u = s.units[j]
                            c = col[:, u.un % 8, :]
                            dve.wait_ge(exp_done, u.exp)
                            if s.g == "C":
                                link(dve.tensor_tensor(c[:, L:L + 1], c[:, L:L + 1], c[:, ES:ES + 1], ALU.add))
                            dve.reciprocal(c[:, R:R + 1], c[:, L:L + 1]).then_inc(r_done, 1)
                            dve.wait_ge(r_done, u.r)
                            pr = pb[:, u.un % PR, 0:u.w]
                            if u.df is None:
                                dve.tensor_scalar(pr, pr, c[:, R:R + 1], None, ALU.mult).then_inc(pnorm_done, 1)
                            else:
                                link(dve.tensor_scalar(c[:, RL:RL + 1], c[:, R:R + 1], lam[:, 5:6], None, ALU.mult))
                                dve.wait_ge(pnorm_done, s.units[j - 1].pn)
                                dve.scalar_tensor_tensor(out=pr, in0=pr, scalar=c[:, RL:RL + 1],
                                                              in1=pb[:, (u.un - 1) % PR, 0:u.w], op0=ALU.mult, op1=ALU.add).then_inc(diff_done, 1)
                        j = i - LAG - 1
                        if 0 <= j < len(s.units) and s.units[j].job.tiles[-1][0] == s.units[j].qt and s.units[j].last:
                            job = s.units[j].job
                            dve.wait_ge(half_done, job.half)
                            dve.wait_ge(o_ready, job.ready)
                            r0 = DH * (job.h % 2)
                            dve.tensor_tensor(z[r0:r0 + DH, job.h // 2, 2 * P * job.qp:2 * P * (job.qp + 1)],
                                                   ob[job.ou % 2][0:DH, 0:2 * P], otmp[:, job.ou % 2, :], ALU.add).then_inc(osum_done, 1)
                        j = i - LAG
                        if 0 <= j < len(s.units) and s.units[j].last:
                            u = s.units[j]
                            qc = (u.qt % 2) * P
                            for p in u.pieces:
                                dve.wait_ge(t_ready, p.tr)
                                lo_sub(pt[:, 1, p.kt:p.kt + p.n, qc:qc + P],
                                       tb[p.tu % 2][:, 0:p.n * P].rearrange("p (t q) -> p t q", t=p.n),
                                       pt[:, 0, p.kt:p.kt + p.n, qc:qc + P], p.lo, p.hi)
                    if s.g == "D":
                        width = TOK if s.l < DEPTH - 1 else S
                        dve.wait_ge(osum_done, s.end_sum)
                        for t, d in enumerate(s.dn):
                            dve.wait_ge(std_done, d.std)
                            dve.scalar_tensor_tensor(out=z[:, t, 0:width], in0=z[:, t, 0:width], scalar=dgain[:, 0:1],
                                                          in1=pb[:, t, 0:width], op0=ALU.mult, op1=ALU.mult).then_inc(cn_done, 1)
                elif s.kind in ("out", "down"):
                    uses = s.uses if s.kind == "out" else [s]
                    gate = 2 * KT if s.kind == "out" else 5 * KT
                    if s.kind == "out":
                        dve.wait_ge(ada_done, plan.ada_at[s.l, gate + KT - 1])
                    for u in uses:
                        dve.wait_ge(big_ready, u.br)
                        if u.x > KT:
                            dve.wait_ge(x_done, u.x - KT)
                        for v, (c0, n) in enumerate(segs(s.width)):
                            xs = x[:, u.m, c0:c0 + n]
                            ins = dve.scalar_tensor_tensor(out=xs, in0=big[u.su % 2][:, c0:c0 + n],
                                                           scalar=ada[:, s.l, gate + u.m, v:v + 1], in1=xs,
                                                           op0=ALU.mult, op1=ALU.add)
                        ins.then_inc(x_done, 1)
                elif s.kind == "up":
                    pa, pc = pb[:, 2 * (s.c % 2), 0:s.width], pb[:, 2 * (s.c % 2) + 1, 0:s.width]
                    dve.wait_ge(relu_done, s.relu)
                    dve.wait_ge(lo_done, s.lo - 2)
                    dve.tensor_tensor(pc, pa, pa, ALU.mult).then_inc(u2_done, 1)
                    dve.wait_ge(u2_done, s.u2)
                    lo_sub(arena[:, CPQ + s.c, 0:s.width], pc, arena[:, s.c, 0:s.width], s.lo, s.hi)

        @block.tensor
        def _(pe):
            def mm(dst, lhs, rhs, start, stop):
                return pe.matmul(dst, lhs, rhs, start=start, stop=stop)

            def dense(dst, wsl, act_hi, act_lo, ks, wcols, width, need=None):
                n = len(ks)
                for i, k in enumerate(ks):
                    if need is not None:
                        pe.wait_ge(lo_done, need[i])
                    wc = wcols(k)
                    for p, (w, a) in enumerate(((w_hi, act_hi), (w_hi, act_lo), (w_lo, act_hi))):
                        for c0, m in segs(width):
                            ins = mm(dst[:, c0:c0 + m], w[:, wsl, wc:wc + P], a(k)[:, c0:c0 + m],
                                     i == 0 and p == 0, i == n - 1 and p == 2)
                return ins

            def plain(dst, terms, width):
                for c0, m in segs(width):
                    for i, (w, a) in enumerate(terms):
                        ins = mm(dst[:, c0:c0 + m], w, a[:, c0:c0 + m], i == 0, i == len(terms) - 1)
                return ins

            def mat(i):
                return mt[:, i, :]

            def b_prep(s):
                pe.wait_ge(group_in, 16 * s.gin)
                uq = gs[:, 0:768].rearrange("p (k c) -> p k c", k=2)
                ukv = gs[:, 768:1280]
                pe.wait_ge(sq_done, s.sq[1])
                if s.ssq_q[0] >= 2:
                    pe.wait_ge(*big_free(s.ssq_q[0]))
                plain(big[s.ssq_q[0] % 2], [(mat(M_ONES), pb[:, 0, :]), (mat(M_ONES)[0:DH], pb[0:DH, 1, :])], s.wq).then_inc(big_ready, 1)
                pe.wait_ge(sq_done, s.sq[2])
                if s.ssq_kv[0] >= 2:
                    pe.wait_ge(*big_free(s.ssq_kv[0]))
                plain(big[s.ssq_kv[0] % 2], [(mat(M_ONES), pb[:, 2, :])], TOK).then_inc(big_ready, 1)
                r = slice(DH, DH + ROPE)
                if s.rep[0] >= 2:
                    pe.wait_ge(*big_free(s.rep[0]))
                plain(big[s.rep[0] % 2], [(mat(M_REP)[r], z[r, 1, :])], TOK).then_inc(big_ready, 1)
                if s.krot[0] >= 2:
                    pe.wait_ge(*t_free(s.krot[0]))
                plain(tb[s.krot[0] % 2], [(mat(M_RROT)[r], z[r, 1, :])], S).then_inc(t_ready, 1)
                pe.wait_ge(cn_done, s.cn[0])
                for t, u in enumerate([s.q[0][0], s.q[1][0], s.qr]):
                    if u[0] >= 2:
                        pe.wait_ge(*big_free(u[0]))
                    c = slice(t * P, (t + 1) * P)
                    plain(big[u[0] % 2], [(uq[:, 0, c], z[:, 0, :]), (uq[0:DH, 1, c], z[0:DH, 1, :])], s.wq).then_inc(big_ready, 1)
                pe.wait_ge(cn_done, s.cn[1])
                for t, (u, _) in enumerate(s.k):
                    if u[0] >= 2:
                        pe.wait_ge(*big_free(u[0]))
                    plain(big[u[0] % 2], [(ukv[:, t * P:(t + 1) * P], z[:, 2, :])], TOK).then_inc(big_ready, 1)
                pe.wait_ge(z_done, s.qz)
                if s.qrot[0] >= 2:
                    pe.wait_ge(*t_free(s.qrot[0]))
                plain(tb[s.qrot[0] % 2], [(mat(M_P32), pb[:, 3, :])], S).then_inc(t_ready, 1)
                for t, (u, _) in enumerate(s.v):
                    if u[0] >= 2:
                        pe.wait_ge(*t_free(u[0]))
                    for j in range(2):
                        c = (2 * t + j) * P
                        ins = mm(tb[u[0] % 2][:, j * 256:(j + 1) * 256], z[:, 2, c:c + P], ukv[:, 256:512], True, True)
                    ins.then_inc(t_ready, 1)

            def operands(g, h, t):
                if g == "A":
                    return [(h // 2, 2 + h // 2, slice(DH * (h % 2), DH * (h % 2) + DH))]
                if g == "C":
                    return [(h % 2, 2, slice(DH * (h // 2), DH * (h // 2) + DH))]
                if g == "B":
                    return [(h // 2, 3 + h // 2, slice(DH * (h % 2), DH * (h % 2) + DH)),
                            (2, 5, slice(ROPE * h, ROPE * h + ROPE))]
                c = 2 * h + t
                return [(c // 4, 2 + c // 4, slice(32 * (c % 4), 32 * (c % 4) + 32))]

            def attn(s):
                pe.wait_ge(lo_done, s.qlo)
                for i in range(len(s.units) + LAG + 1):
                    if i < len(s.units):
                        u = s.units[i]
                        if u.su >= 2:
                            pe.wait_ge(*big_free(u.su))
                        q = slice(u.qt * P, (u.qt + 1) * P)
                        parts = [(S, S + C, S)] + ([(S - u.wl, S, u.loc[0] * P)] if u.loc else [])
                        for a, b, k0 in parts:
                            ops = [(qk(qs, qp)[r, q], qk(ks, kp)[r, k0:k0 + b - a])
                                   for qs, ks, r in operands(s.g, u.h, u.t) for qp, kp in ((0, 0), (1, 0), (0, 1))]
                            for n, (w, m) in enumerate(ops):
                                ins = mm(big[u.su % 2][:, a:b], w, m, n == 0, n == len(ops) - 1)
                        ins.then_inc(big_ready, 1)
                    j = i - LAG - 1
                    if 0 <= j < len(s.units) and s.units[j].job.tiles[-1][0] == s.units[j].qt and s.units[j].last:
                        job = s.units[j].job
                        pe.wait_ge(lo_done, s.units[j].pieces[-1].lo)
                        if job.ou >= 2:
                            pe.wait_ge(osum_done, plan.o_free[job.ou - 2])
                        hv = job.h // 2 if s.g == "C" else job.h
                        kts = [4, 5] + sorted({k for _, loc in job.tiles for k in loc})
                        for n, kt in enumerate(kts):
                            cols = [qt % 2 for qt, loc in job.tiles if kt >= 4 or kt in loc]
                            c = slice(cols[0] * P, (cols[-1] + 1) * P)
                            for part in range(2):
                                ins = mm(ob[job.ou % 2][:, c], vals[:, kt, hv, :, :].rearrange("p s d -> p (s d)"),
                                         pt[:, part, kt, c], n == 0 and part == 0, n == len(kts) - 1 and part == 1)
                        ins.then_inc(o_ready, 1)
                    j = i - LAG
                    if 0 <= j < len(s.units) and s.units[j].last:
                        u = s.units[j]
                        if u.df:
                            pe.wait_ge(diff_done, u.df)
                        else:
                            pe.wait_ge(pnorm_done, u.pn)
                        for p in u.pieces:
                            if p.tu >= 2:
                                pe.wait_ge(*t_free(p.tu))
                            for n in range(p.n):
                                c = p.col + n * P
                                ins = pe.transpose(tb[p.tu % 2][:, n * P:(n + 1) * P], pb[:, u.un % PR, c:c + P], mat(M_ID))
                            ins.then_inc(t_ready, 1)
                if s.g == "D":
                    for t, d in enumerate(s.dn):
                        width = TOK if s.l < DEPTH - 1 else S
                        pe.wait_ge(sq_done, d.sq)
                        if d.su >= 2:
                            pe.wait_ge(*big_free(d.su))
                        plain(big[d.su % 2], [(mat(M_BONES), pb[:, t, :])], width).then_inc(big_ready, 1)

            pe.wait_ge(const_in, 16 * 5)
            pe.wait_ge(silu_done, 1)
            for s in steps:
                if s.kind == "ada":
                    pe.wait_ge(raw_in[s.n % RAW], 16 * (s.n // RAW + 1))
                    if s.tu >= 2:
                        pe.wait_ge(*t_free(s.tu))
                    for k in range(KT):
                        ins = mm(tb[s.tu % 2][:, 0:2], raw[:, s.n % RAW, k * P:(k + 1) * P], cs[:, k, :], k == 0, k == KT - 1)
                    ins.then_inc(t_ready, 1)
                elif s.kind == "norm":
                    pe.wait_ge(acc_done, s.acc)
                    if s.su >= 2:
                        pe.wait_ge(*big_free(s.su))
                    plain(big[s.su % 2], [(mat(M_ONES), z[:, 2, :])], s.width).then_inc(big_ready, 1)
                elif s.kind == "in":
                    pe.wait_ge(split_done, s.b.i)
                    if s.su >= 2:
                        pe.wait_ge(*big_free(s.su))
                    ins = dense(big[s.su % 2], (s.b.i - 1) % WR, lambda k: h_hi[:, k, :], lambda k: h_lo[:, k, :], range(KT),
                                lambda k: k * P, s.width, [hh[2] for hh in s.hs])
                    ins.then_inc(big_ready, 1)
                elif s.kind == "vpost":
                    pe.wait_ge(z_done, s.zd)
                    for p in s.pieces:
                        if p.tu >= 2:
                            pe.wait_ge(*t_free(p.tu))
                        for j in range(p.n):
                            kt = p.kt + j
                            ins = pe.transpose(tb[p.tu % 2][:, j * P:(j + 1) * P], z[:, s.z, kt * P:(kt + 1) * P], mat(M_ID))
                        ins.then_inc(t_ready, 1)
                elif s.kind == "rope":
                    pe.wait_ge(z_done, s.zd)
                    if s.tu >= 2:
                        pe.wait_ge(*t_free(s.tu))
                    plain(tb[s.tu % 2], [(mat(M_P64 if s.g == "C" else M_P32), z[:, s.z, :])], S).then_inc(t_ready, 1)
                elif s.kind == "bprep":
                    b_prep(s)
                elif s.kind == "attn":
                    attn(s)
                elif s.kind == "out":
                    pe.wait_ge(split_done, s.b.i)
                    pe.wait_ge(mix_done, s.mix)
                    for k, u in enumerate(s.uses):
                        if u.su >= 2:
                            pe.wait_ge(*big_free(u.su))
                        ins = dense(big[u.su % 2], (s.b.i - 1) % WR, lambda kk: mix_hi[:, kk, :], lambda kk: mix_lo[:, kk, :],
                                    range(2), lambda kk: kk * 4 * P + k * P, s.width)
                        ins.then_inc(big_ready, 1)
                elif s.kind == "up":
                    pe.wait_ge(split_done, s.b.i)
                    if s.su >= 2:
                        pe.wait_ge(*big_free(s.su))
                    ins = dense(big[s.su % 2], (s.b.i - 1) % WR, lambda k: h_hi[:, k, :], lambda k: h_lo[:, k, :], range(KT),
                                lambda k: k * P, s.width, [hh[2] for hh in s.hs])
                    ins.then_inc(big_ready, 1)
                elif s.kind == "down":
                    pe.wait_ge(split_done, s.b.i)
                    if s.su >= 2:
                        pe.wait_ge(*big_free(s.su))
                    ins = dense(big[s.su % 2], (s.b.i - 1) % WR, lambda k: arena[:, k, :], lambda k: arena[:, CPQ + k, :],
                                range(CPQ), lambda k: k * P, s.width, s.us)
                    ins.then_inc(big_ready, 1)



def _matrices():
    m = np.zeros((P, 7, P), np.float32)
    m[:, M_ID] = np.eye(P)
    m[:, M_ONES] = 1.0
    m[:, M_BONES] = np.kron(np.eye(2), np.ones((DH, DH)))

    def rot(n):
        r = np.zeros((n, n), np.float32)
        for d in range(n // 2):
            r[d + n // 2, d] = -1.0
            r[d, d + n // 2] = 1.0
        return r

    m[:, M_P64] = np.kron(np.eye(2), rot(64))
    m[:, M_P32] = np.kron(np.eye(4), rot(32))
    m[DH:DH + ROPE, M_REP] = np.tile(np.eye(ROPE), (1, HEADS))
    m[DH:DH + ROPE, M_RROT] = np.tile(rot(ROPE), (1, HEADS))
    return m


def _rope_table(dim):
    nf = dim // 4
    freqs = (np.float32(ROPE_BASE) ** (-np.arange(nf, dtype=np.float32) / np.float32(nf))).astype(np.float32)
    t = np.arange(S)
    row, column = (t // GRID_W).astype(np.float32), (t % GRID_W).astype(np.float32)
    ang = np.concatenate([row[:, None] * freqs, column[:, None] * freqs], axis=1).astype(np.float32)
    f = np.arange(P) % (dim // 2)
    return np.stack([np.cos(ang)[:, f].T, np.sin(ang)[:, f].T], axis=1).astype(np.float32)


def _column_mask():
    qc = np.arange(P) % GRID_W
    c0 = np.clip(qc - NA_COLS // 2, 0, GRID_W - NA_COLS)[:, None]
    kc = np.arange(GRID_W)[None, :]
    return np.where((kc >= c0) & (kc < c0 + NA_COLS), 0.0, NEG).astype(np.float32)


def _window_mask():
    q, k = np.arange(P)[:, None], np.arange(P)[None, :]
    return np.concatenate([np.where(k >= q, 0.0, NEG), np.zeros((P, P)), np.where(k <= q, 0.0, NEG)], axis=1).astype(np.float32)



def _cols(v):
    return v.reshape(-1, P).T


def _vectors(b_ada, norm_attn_g, norm_mlp_g, mla_q_norm_g, mla_kv_norm_g, diff_norm_g, swa_sink, diff_lambda):
    v = np.zeros((P, DEPTH, V_LEN), np.float32)
    for l in range(DEPTH):
        v[:, l, V_BADA:V_BADA + NADA] = _cols(b_ada[l])
        v[:, l, V_GATTN:V_GATTN + KT] = _cols(norm_attn_g[l])
        v[:, l, V_GMLP:V_GMLP + KT] = _cols(norm_mlp_g[l])
        v[:, l, V_GQ] = mla_q_norm_g[l, 0:P]
        v[0:QLORA - P, l, V_GQ + 1] = mla_q_norm_g[l, P:]
        v[:, l, V_GKV] = mla_kv_norm_g[l]
        v[:, l, V_DNG] = np.concatenate([diff_norm_g[l]] * 2)
        v[:, l, V_SINK:V_SINK + HEADS] = swa_sink[l][None, :]
        v[:, l, V_LAM:V_LAM + 128] = diff_lambda[l].reshape(1, -1)
    return v


def _w_in_blocks(w):
    a, b, c, d = 0, 768, 1120, 1632
    order = list(range(a, a + 768))
    order += list(range(b, b + QLORA)) + list(range(b + 320, b + 352)) + [-1] * 32 + list(range(b + QLORA, b + 320))
    for h in (0, 2, 1, 3):
        order += list(range(c + DH * h, c + DH * (h + 1)))
    order += list(range(c + 256, c + 512)) + list(range(d, d + 768))
    padded = np.concatenate([w, np.zeros_like(w[:, :, :1])], axis=2)
    return np.ascontiguousarray(
        padded[:, :, order].reshape(DEPTH, KT, P, NIN, P).transpose(0, 3, 2, 1, 4)).reshape(DEPTH, NIN, P, D)


def _blocks(w, n):
    return np.ascontiguousarray(w.reshape(DEPTH, KT, P, n, P).transpose(0, 3, 2, 1, 4)).reshape(DEPTH, n, P, D)


def _rpb_windows(rpb):
    qc, kc = np.arange(GRID_W)[:, None], np.arange(GRID_W)[None, :]
    dc = np.clip(kc - qc + NA_COLS - 1, 0, 2 * NA_COLS - 2)
    win = rpb[:, :, :, dc].transpose(0, 1, 3, 2, 4)
    pad = np.zeros_like(win[:, :, :, :1])
    both = np.stack([np.concatenate([win, pad], axis=3), np.concatenate([pad, win], axis=3)], axis=2)
    return np.ascontiguousarray(both).reshape(DEPTH, HEADS, P, 1024)


def kernel(x, c, ctx, c_ctx, w_ada, b_ada, norm_attn_g, w_in, na_rpb, mla_q_norm_g, mla_w_uq, mla_kv_norm_g, mla_w_ukv,
           swa_sink, diff_lambda, diff_norm_g, w_out, norm_mlp_g, w_up, w_down, final_norm_g):
    import concourse.bacc as bacc
    from concourse.bass_utils import run_bass_kernel_spmd

    a = {k: np.asarray(v) for k, v in dict(
        x=x, c=c, ctx=ctx, c_ctx=c_ctx, w_ada=w_ada, b_ada=b_ada, norm_attn_g=norm_attn_g, w_in=w_in, na_rpb=na_rpb,
        mla_q_norm_g=mla_q_norm_g, mla_w_uq=mla_w_uq, mla_kv_norm_g=mla_kv_norm_g, mla_w_ukv=mla_w_ukv, swa_sink=swa_sink,
        diff_lambda=diff_lambda, diff_norm_g=diff_norm_g, w_out=w_out, norm_mlp_g=norm_mlp_g, w_up=w_up, w_down=w_down,
        final_norm_g=final_norm_g).items()}
    tokens = np.concatenate([a["x"][0], a["ctx"][0]], axis=0)
    nope = [h * 96 + i for h in range(HEADS) for i in range(DH)]
    rope = [h * 96 + DH + i for h in range(HEADS) for i in range(ROPE)]
    uq = np.concatenate([a["mla_w_uq"], np.zeros((DEPTH, 2 * P - QLORA, 384), np.float32)], axis=1)[:, :, nope + rope]
    kcols = [h * P + i for h in range(HEADS) for i in range(DH)]
    vcols = [h * P + DH + i for h in range(HEADS) for i in range(DH)]
    wo = a["w_out"].reshape(DEPTH, 4, 2, P, 2, 4, P)
    arrays = {
        "xt": tokens.T.reshape(KT, P, TOK).transpose(1, 0, 2),
        "cvec": np.stack([_cols(a["c"][0]), _cols(a["c_ctx"])], axis=2),
        "vecs": _vectors(a["b_ada"], a["norm_attn_g"], a["norm_mlp_g"], a["mla_q_norm_g"], a["mla_kv_norm_g"],
                         a["diff_norm_g"], a["swa_sink"], a["diff_lambda"]),
        "gfin": _cols(a["final_norm_g"]),
        "mats": _matrices(),
        "rope": np.stack([_rope_table(64), _rope_table(32)]),
        "maskna": _column_mask(),
        "masksw": _window_mask(),
        "rpb": _rpb_windows(a["na_rpb"]),
        "wuq": uq.reshape(DEPTH, 2, P, 384).transpose(0, 2, 1, 3).reshape(DEPTH, P, 768),
        "wukv": a["mla_w_ukv"][:, :, kcols + vcols],
        "w_ada": _blocks(a["w_ada"], NADA),
        "w_in": _w_in_blocks(a["w_in"]),
        "w_out": wo.transpose(0, 1, 4, 3, 2, 5, 6).reshape(DEPTH, 8, P, D),
        "w_up": _blocks(a["w_up"], NCHUNK),
        "w_down": a["w_down"].reshape(DEPTH, NQ, CPQ, P, KT, P).transpose(0, 1, 4, 3, 2, 5).reshape(DEPTH, NQ * KT, P, D),
    }
    arrays = {k: np.ascontiguousarray(v) for k, v in arrays.items()}
    nc = bacc.Bacc("TRN2", target_bir_lowering=False, num_devices=1, dynamic_dma_scratch_size=1024)
    args = {k: nc.dram_tensor(k + "_dram", v.shape, F32, kind="ExternalInput").ap() for k, v in arrays.items()}
    out = nc.dram_tensor("out_dram", (P, KT, S), F32, kind="ExternalOutput").ap()
    build_program(nc, out=out, **args)
    r = run_bass_kernel_spmd(nc, [{k + "_dram": v for k, v in arrays.items()}], core_ids=[0])
    got = r.results[0]["out_dram"]
    return got.transpose(2, 1, 0).reshape(1, S, D)
```

```python
from contextlib import ExitStack

import numpy as np

import concourse.bass as bass
from concourse import mybir

P = 128
D = 1024
KT = D // P
S, C = 512, 256
TOK = S + C
DEPTH = 2
HEADS, DH = 4, 64
GRID_W = 64
NA_COLS = 16
QLORA, KVLORA, ROPE = 192, 128, 32
NCHUNK = 32
NQ = 4
CPQ = NCHUNK // NQ
NADA = 6 * KT
ACOLS = 512
AHC = 6 * D // ACOLS
AKB = D // (2 * P)
EPS = 1e-6
NEG = -1e30
LOWEST = -3.0e38
ROPE_BASE = 10000.0
LAM_INIT = [0.8 - 0.6 * float(np.exp(-0.3 * l)) for l in range(DEPTH)]

GROUPS = "ACBD"
TILES = {
    "A": [("q", 0), ("q", 1), ("k", 2), ("k", 3), ("v", 0), ("v", 1)],
    "B": [("cq", 0), ("cqkr", 1), ("ckv", 2)],
    "C": [("qr", 0), ("qr", 1), ("kr", 2), ("v", 0)],
    "D": [("qr", 0), ("qr", 1), ("kr", 2), ("kr", 3), ("v", 0), ("v", 1)],
}
TILE0 = {"A": 0, "B": 6, "C": 9, "D": 13}
NIN = 19
MIX0 = {"A": 0, "B": 2, "C": 4, "D": 6}
SCALE = {"A": DH ** -0.5, "B": (DH + ROPE) ** -0.5, "C": DH ** -0.5, "D": (DH // 2) ** -0.5}

V_BADA, V_GATTN, V_GMLP, V_GQ, V_GKV, V_DNG, V_SINK, V_LAM = 0, 48, 56, 64, 66, 67, 68, 72
V_LEN = 72 + 128
M_ID, M_ONES, M_BONES, M_P64, M_P32, M_REP, M_RROT = range(7)

RAW, WR, ZR, PR = 3, 3, 3, 4
LAG = 3

F32 = mybir.dt.float32
F32R = mybir.dt.float32r
ALU = mybir.AluOpType
ACT = mybir.ActivationFunctionType
AXX = mybir.AxisListType.X


def segs(width):
    return [(0, S)] + ([(S, C)] if width > S else [])


class Step:

    def __init__(self, kind=None, acc=None, b=None, br=None, c=None, col=None, comps=None, done=None, first=None,
                 g=None, gin=None, h=None, hb=None, hi=None, hs=None, i=None, j=None, job=None, jobs=None, kt=None,
                 l=None, last=None, lo=None, loc=None, m=None, mix=None, mul=None, n=None, pieces=None, qlo=None,
                 qp=None, qt=None, relu=None, slot=None, sq=None, std=None, su=None, sum=None, t=None, tiles=None,
                 tr=None, tu=None, u2=None, un=None, units=None, us=None, uses=None, what=None, which=None, width=None,
                 wl=None, wq=None, x=None, z=None, zd=None):
        self.kind = kind
        self.acc = acc
        self.b = b
        self.br = br
        self.c = c
        self.col = col
        self.comps = comps
        self.done = done
        self.first = first
        self.g = g
        self.gin = gin
        self.h = h
        self.hb = hb
        self.hi = hi
        self.hs = hs
        self.i = i
        self.j = j
        self.job = job
        self.jobs = jobs
        self.kt = kt
        self.l = l
        self.last = last
        self.lo = lo
        self.loc = loc
        self.m = m
        self.mix = mix
        self.mul = mul
        self.n = n
        self.pieces = pieces
        self.qlo = qlo
        self.qp = qp
        self.qt = qt
        self.relu = relu
        self.slot = slot
        self.sq = sq
        self.std = std
        self.su = su
        self.sum = sum
        self.t = t
        self.tiles = tiles
        self.tr = tr
        self.tu = tu
        self.u2 = u2
        self.un = un
        self.units = units
        self.us = us
        self.uses = uses
        self.what = what
        self.which = which
        self.width = width
        self.wl = wl
        self.wq = wq
        self.x = x
        self.z = z
        self.zd = zd


class Plan:

    def __init__(self):
        self.n = {}
        self.raw = []
        self.raw_free = []
        self.big_free = []
        self.t_free = []
        self.o_free = []
        self.z_free = [[] for _ in range(ZR)]
        self.nz = 0
        self.steps = []
        self.build()

    def tick(self, name):
        self.n[name] = self.n.get(name, 0) + 1
        return self.n[name]

    def add(self, kind, **kw):
        s = Step(kind=kind, **kw)
        self.steps.append(s)
        return s

    def big(self):
        self.big_free.append(None)
        return len(self.big_free) - 1, self.tick("big_ready")

    def tbank(self):
        self.t_free.append(None)
        return len(self.t_free) - 1, self.tick("t_ready")

    def wblock(self, name, l, idx):
        b = Step(i=self.tick("split_done"))
        b.source = (name, l, idx)
        return b

    def hilo(self):
        return self.tick("hi_done"), self.tick("lo_done")

    def ada(self, l, count, where, double=False):
        for _ in range(count):
            i = self.ada_next[l]
            if i >= AHC * AKB:
                return
            self.ada_next[l] += 1
            if not double:
                self.ada_sum()
            s = self.add("ada", l=l, i=i, j=i // AKB, kt=2 * (i % AKB))
            s.where, s.par = where, (s.j // 2 % 2 if double else 1)
            s.part = self.tick("ada_part")
            s.lo_before = self.n.get("lo_done", 0)
            if double:
                self.ada_sum()
            if i % AKB == AKB - 1:
                self.ada_pending = s

    def ada_sum(self):
        s, self.ada_pending = self.ada_pending, None
        if s is None:
            return
        tu, tr = self.tbank()
        done = self.tick("ada_done")
        self.t_free[tu] = ("ada_done", done)
        for t in range(ACOLS // P):
            self.ada_at[s.l, s.j * (ACOLS // P) + t] = done
        a = self.add("adasum", l=s.l, j=s.j, tu=tu, tr=tr, done=done)
        a.where, a.par, a.part = s.where, s.par, s.part

    def ssq(self, m, width):
        a = self.tick("sq_done")
        d = self.tick("acc_done") if m else None
        self.add("ssq", m=m, width=width, sq=a, acc=d).pool = False

    def stat(self, width):
        su, br = self.big()
        std = self.tick("std_done")
        self.big_free[su] = ("std_done", std)
        self.add("stat", width=width, su=su, br=br, std=std, acc=self.n["acc_done"])
        return std

    def norm(self, l, which, width, std):
        hs = []
        for _ in range(KT):
            if which == "final":
                hs.append(self.tick("y_done"))
            else:
                t = self.tick("t_done")
                hs.append((t, *self.hilo()))
        self.h_at = hs
        self.z_free = [[] for _ in range(ZR)]
        self.add("norm", l=l, which=which, width=width, std=std, hs=hs)

    def zslot(self):
        z = self.nz % ZR
        self.nz += 1
        w, self.z_free[z] = self.z_free[z], []
        return z, w

    def inproj(self, l, g, last):
        self.nz = 0
        self.gin += {"A": 0, "C": 2, "B": 3, "D": 0}[g]
        post = []
        for j, (what, slot) in enumerate(TILES[g]):
            if l == 0:
                self.ada(0, {"A": (2, 2, 1, 1, 1, 1), "C": (1, 1, 1, 1), "B": (2, 1, 1), "D": (2, 2, 1, 1, 1, 1)}[g][j], "pb")
            width = S if (l == DEPTH - 1 and what in ("q", "qr", "cq")) else TOK
            b = self.wblock("in", l, TILE0[g] + j)
            su, br = self.big()
            b.end = br
            st = self.add("in", l=l, g=g, b=b, su=su, br=br, what=what, slot=slot, width=width, first=(j == 0), hs=self.h_at)
            if what in ("q", "k"):
                st.hi, st.lo = self.hilo()
                self.big_free[su] = ("lo_done", st.lo)
            else:
                st.z, st.zwait = self.zslot()
                st.zd = self.tick("z_done")
                self.big_free[su] = ("z_done", st.zd)
            if j == 0 and last is not None:
                self.outproj(l, last)
            for p in post:
                self.post(*p)
            post = [(l, g, what, slot, width, st)] if what in ("v", "qr", "kr") else []
        self.ada_sum()
        for p in post:
            self.post(*p)
        if g == "B":
            self.bprep(l)

    def post(self, l, g, what, slot, width, src):
        if what == "v":
            pieces = []
            for kt, n in ((0, 4), (4, 2)):
                tu, tr = self.tbank()
                hi, lo = self.hilo()
                self.t_free[tu] = ("lo_done", lo)
                pieces.append(Step(kt=kt, n=n, tu=tu, tr=tr, hi=hi, lo=lo))
            self.z_free[src.z] = [("t_ready", pieces[-1].tr)]
            self.add("vpost", slot=slot, z=src.z, zd=src.zd, pieces=pieces)
        else:
            tu, tr = self.tbank()
            mul = self.tick("rope_done")
            rs = self.tick("rope_done")
            hi, lo = self.hilo()
            self.t_free[tu] = ("rope_done", mul)
            self.z_free[src.z] = [("lo_done", lo)]
            self.add("rope", g=g, gin=self.gin, slot=slot, z=src.z, zd=src.zd, width=width, tu=tu, tr=tr, mul=mul, sum=rs, hi=hi, lo=lo)

    def bprep(self, l):
        wq = S if l == DEPTH - 1 else TOK
        s = self.add("bprep", l=l, gin=self.gin, wq=wq, zd=self.n["z_done"])
        s.ada_before = self.n["ada_done"]
        s.sq = [self.tick("sq_done") for _ in range(3)]
        s.ssq_q, s.ssq_kv = self.big(), self.big()
        s.std = [self.tick("std_done") for _ in range(2)]
        self.big_free[s.ssq_q[0]] = ("std_done", s.std[0])
        self.big_free[s.ssq_kv[0]] = ("std_done", s.std[1])
        s.cn = [self.tick("cn_done") for _ in range(2)]
        s.rep, s.krot = self.big(), self.tbank()
        s.krope = self.tick("rope_done")
        self.big_free[s.rep[0]] = ("rope_done", s.krope)
        self.t_free[s.krot[0]] = ("rope_done", s.krope)
        s.khl = self.hilo()
        s.q = []
        for _ in range(2):
            u = self.big()
            hl = self.hilo()
            self.big_free[u[0]] = ("lo_done", hl[1])
            s.q.append((u, hl))
        s.qr = self.big()
        s.qz = self.tick("z_done")
        self.big_free[s.qr[0]] = ("z_done", s.qz)
        s.k = []
        for _ in range(2):
            u = self.big()
            hl = self.hilo()
            self.big_free[u[0]] = ("lo_done", hl[1])
            s.k.append((u, hl))
        s.qrot = self.tbank()
        s.qmul = self.tick("rope_done")
        s.qrope = self.tick("rope_done")
        self.t_free[s.qrot[0]] = ("rope_done", s.qmul)
        s.qhl = self.hilo()
        s.v = []
        for _ in range(3):
            u = self.tbank()
            hl = self.hilo()
            self.t_free[u[0]] = ("lo_done", hl[1])
            s.v.append((u, hl))

    def attention(self, l, g):
        units, jobs = [], []
        comps = 2 if g == "D" else 1
        last_qt = 6 if l < DEPTH - 1 else 4
        qlo = self.n["lo_done"]
        for h in range(HEADS):
            for qp in range(last_qt // 2):
                job = Step(h=h, qp=qp, tiles=[])
                for qt in (2 * qp, 2 * qp + 1):
                    if qt >= 4:
                        loc = []
                    elif g == "C":
                        loc = list(range(max(0, qt - 1), min(3, qt + 1) + 1))
                    else:
                        loc = list(range(4))
                    for t in range(comps):
                        u = Step(h=h, qt=qt, t=t, loc=loc, wl=len(loc) * P, job=job, un=self.nu,
                                 pieces=[], last=(t == comps - 1))
                        self.nu += 1
                        u.w = u.wl + C
                        u.biased = g in "AC" and bool(loc)
                        units.append(u)
                        job.tiles.append((qt, loc)) if u.last else None
                jobs.append(job)
        st = self.add("attn", l=l, g=g, gin=self.gin, units=units, jobs=jobs, qlo=qlo, comps=comps)
        st.ada_before = self.n["ada_done"]
        for i in range(len(units) + LAG + 1):
            if i < len(units):
                u = units[i]
                u.su, u.br = self.big()
                if u.biased:
                    u.bias = [self.tick("bias_done"), self.tick("bias_done")]
                u.nm = self.tick("nmax_done")
                u.exp = self.tick("exp_done")
                self.big_free[u.su] = ("bias_done", u.bias[1]) if u.biased else ("exp_done", u.exp)
                u.r = self.tick("r_done")
                u.pn = self.tick("pnorm_done") if not (g == "D" and u.t == 1) else None
                u.df = self.tick("diff_done") if g == "D" and u.t == 1 else None
            j = i - LAG - 1
            if 0 <= j < len(units) and units[j].last and units[j].job.tiles[-1][0] == units[j].qt:
                job = units[j].job
                self.o_free.append(None)
                job.ou = len(self.o_free) - 1
                job.ready = self.tick("o_ready")
                job.half = self.tick("half_done")
                job.sum = self.tick("osum_done")
                self.o_free[job.ou] = job.sum
            j = i - LAG
            if 0 <= j < len(units) and units[j].last:
                u = units[j]
                parts = ([(u.loc[0], len(u.loc), 0)] if u.loc else []) + [(4, 2, u.wl)]
                for kt, n, col in parts:
                    tu, tr = self.tbank()
                    hi, lo = self.hilo()
                    self.t_free[tu] = ("lo_done", lo)
                    u.pieces.append(Step(kt=kt, n=n, col=col, tu=tu, tr=tr, hi=hi, lo=lo))
        st.end_o = self.n["o_ready"]
        st.end_sum = self.n["osum_done"]
        if g == "D":
            st.dn = []
            for t in range(2):
                d = Step(sq=self.tick("sq_done"))
                d.su, d.br = self.big()
                d.std = self.tick("std_done")
                self.big_free[d.su] = ("std_done", d.std)
                d.done = self.tick("cn_done")
                st.dn.append(d)
        st.mix = [self.tick("mix_done") for _ in range(2)]
        st.prev_out = self.last_out
        for z in range(ZR):
            self.z_free[z] = [("mix_done", st.mix[1])]
        return st

    def mlp(self, l):
        width = TOK if l < DEPTH - 1 else S
        for qd in range(NQ):
            us = []
            for c in range(CPQ):
                if l + 1 < DEPTH:
                    self.ada(*((l, 1, "gs") if qd == 0 else (l + 1, 1, "gs")))
                b = self.wblock("up", l, qd * CPQ + c)
                su, br = self.big()
                relu = self.tick("relu_done")
                self.big_free[su] = ("relu_done", relu)
                u2 = self.tick("u2_done")
                hi, lo = self.hilo()
                us.append(lo)
                b.end = br
                self.add("up", l=l, b=b, c=c, su=su, br=br, relu=relu, u2=u2, hi=hi, lo=lo, width=width, hs=self.h_at)
            if qd == 0:
                self.ada_sum()
            for m in range(KT):
                if l + 1 < DEPTH:
                    self.ada(l + 1, 1, "gs")
                b = self.wblock("down", l, qd * KT + m)
                su, br = self.big()
                x = self.tick("x_done")
                self.big_free[su] = ("x_done", x)
                b.end = br
                self.add("down", l=l, b=b, m=m, su=su, br=br, x=x, us=us, width=width)
                if qd == NQ - 1:
                    self.ssq(m, width)
                    self.steps[-1].after = x
        self.ada_sum()

    def build(self):
        self.nu = 0
        self.gin = 0
        self.ada_next = [0] * DEPTH
        self.ada_at = {}
        self.ada_pending = None
        self.last_out = None
        for m in range(KT):
            self.ssq(m, TOK)
            self.steps[-1].after, self.steps[-1].pool = None, True
        for pair in range(2):
            for kb in range(AKB):
                self.ada(0, 1, "pb", double=True)
                if kb == 0:
                    tu, tr = self.tbank()
                s = self.add("adamm", l=0, j=2 * pair + 1, i=(2 * pair + 1) * AKB + kb, kt=2 * kb, tu=tu, tr=tr)
                s.last = kb == AKB - 1
                s.freed = ("t_ready", tr) if s.last else ("ada_mm", self.tick("ada_mm"))
            s.done = self.tick("ada_done")
            self.t_free[tu] = ("ada_done", s.done)
            for t in range(ACOLS // P):
                self.ada_at[0, s.j * (ACOLS // P) + t] = s.done
            self.ada_next[0] += AKB
            if pair == 0:
                std = self.stat(TOK)
        self.ada_sum()
        for l in range(DEPTH):
            self.norm(l, "attn", TOK, std)
            st = None
            for g in GROUPS:
                self.inproj(l, g, st)
                st = self.attention(l, g)
            self.outproj(l, st)
            width = TOK if l < DEPTH - 1 else S
            self.norm(l, "mlp", width, self.stat(width))
            self.mlp(l)
            std = self.stat(width)
        self.norm(DEPTH - 1, "final", S, std)
        for s in self.steps:
            s.pair, s.paired = None, False
        for n, s in enumerate(self.steps):
            if s.kind == "norm" and s.which != "final":
                a, b = [u for u in self.steps[n + 1:] if u.kind in ("in", "up")][0:2]
                a.pair, b.paired = b, True
        blocks = [s.b for s in self.steps if s.kind in ("in", "out", "up", "down")]
        users = [s for s in self.steps if s.kind in ("in", "out", "up", "down")]
        for s in self.steps:
            s.ahead = []
        for i, s in enumerate(users):
            s.ahead = [] if i == 0 else blocks[i + 2:i + 3]
        first_norm = [s for s in self.steps if s.kind == "norm"][0]
        first_norm.ahead = blocks[0:3]
        for b in blocks:
            b.before = blocks[b.i - 1 - WR].end if b.i > WR else 0
        for s in self.steps:
            if s.kind == "ada":
                s.n = len(self.raw)
                self.raw.append(("ada", s.l, s.i))
                self.raw_free.append(("ada_part", s.part))
            if s.kind == "adamm":
                s.n = len(self.raw)
                self.raw.append(("ada", s.l, s.i))
                self.raw_free.append(s.freed)
            for b in s.ahead:
                b.n = len(self.raw)
                self.raw.append(b.source)
                self.raw_free.append(("split_done", b.i))
            s.loads = len(self.raw)

    def outproj(self, l, st):
        g = st.g
        width = TOK if l < DEPTH - 1 else S
        for hb in range(2):
            b = self.wblock("out", l, MIX0[g] + hb)
            uses = []
            for mm in range(4):
                su, br = self.big()
                x = self.tick("x_done")
                self.big_free[su] = ("x_done", x)
                uses.append(Step(m=4 * hb + mm, su=su, br=br, x=x))
            b.end = uses[-1].br
            self.add("out", l=l, g=g, b=b, hb=hb, uses=uses, width=width, mix=st.mix[1])
            if g == GROUPS[-1]:
                for u in uses:
                    self.ssq(u.m, width)
                    self.steps[-1].after = u.x
            self.last_out = uses[-1].br


def build_program(nc, xt, cvec, vecs, gfin, mats, rope, maskna, masksw, rpb, wuq, wukv,
                  w_ada, w_in, w_out, w_up, w_down, out):
    plan = Plan()
    dram = {"ada": w_ada, "in": w_in, "out": w_out, "up": w_up, "down": w_down}
    steps = plan.steps

    with ExitStack() as ctx:
        def sb(name, shape, dt=F32):
            return ctx.enter_context(nc.sbuf_tensor(name, shape, dt))

        x = sb("x", [P, KT, TOK])
        h_hi, h_lo = sb("h_hi", [P, KT, TOK], F32R), sb("h_lo", [P, KT, TOK], F32R)
        arena = sb("arena", [P, 16, TOK], F32R)
        pt = sb("pt", [P, 2, 6, 2 * P], F32R)
        raw = sb("raw", [P, RAW, D])
        w_hi, w_lo = sb("w_hi", [P, WR, D], F32R), sb("w_lo", [P, WR, D], F32R)
        z = sb("z", [P, ZR, TOK])
        gs = sb("gs", [P, 2048])
        pb = sb("pb", [P, PR, TOK])
        mix_hi, mix_lo = sb("mix_hi", [P, 2, TOK], F32R), sb("mix_lo", [P, 2, TOK], F32R)
        rt = sb("rt", [P, 2, S])
        mt = sb("mt", [P, 7, P])
        mna = sb("mna", [P, GRID_W])
        zeros = sb("zeros", [P, C])
        vec = sb("vec", [P, DEPTH, V_LEN])
        gf = sb("gf", [P, KT])
        cv, cs = sb("cv", [P, KT, 2]), sb("cs", [P, KT, 2])
        ada = sb("ada", [P, DEPTH, NADA, 2])
        amul = sb("amul", [P, KT, 2])
        otmp = sb("otmp", [DH, 2, 2 * P])
        col = sb("col", [P, 8, 8])
        eps = sb("eps", [P, 1])
        lam = sb("lam", [P, 8])
        nsink = sb("nsink", [P, HEADS])
        dgain = sb("dgain", [P, 1])
        MX, MX2, NM, L, ES, R, RL = range(7)

        big = [ctx.enter_context(nc.psum_tensor(f"big{i}", [P, 1024], F32)) for i in range(2)]
        tb = [ctx.enter_context(nc.psum_tensor(f"tb{i}", [P, 512], F32)) for i in range(2)]
        ob = [ctx.enter_context(nc.psum_tensor(f"ob{i}", [P, 512], F32)) for i in range(2)]

        def semaphore(name):
            return ctx.enter_context(nc.semaphore(name))

        acc_done = semaphore("acc_done")
        ada_done = semaphore("ada_done")
        ada_part = semaphore("ada_part")
        ada_mm = semaphore("ada_mm")
        bias_done = semaphore("bias_done")
        big_ready = semaphore("big_ready")
        cexp_done = semaphore("cexp_done")
        cn_done = semaphore("cn_done")
        const_in = semaphore("const_in")
        diff_done = semaphore("diff_done")
        dve_step = semaphore("dve_step")
        exp_done = semaphore("exp_done")
        group_in = semaphore("group_in")
        half_done = semaphore("half_done")
        hi_done = semaphore("hi_done")
        hi_split = semaphore("hi_split")
        lam_dot = semaphore("lam_dot")
        lam_exp = semaphore("lam_exp")
        ln_done = semaphore("ln_done")
        lo_done = semaphore("lo_done")
        mix_done = semaphore("mix_done")
        mix_half = semaphore("mix_half")
        nmax_done = semaphore("nmax_done")
        o_ready = semaphore("o_ready")
        osum_done = semaphore("osum_done")
        pnorm_done = semaphore("pnorm_done")
        r_done = semaphore("r_done")
        relu_done = semaphore("relu_done")
        rope_done = semaphore("rope_done")
        silu_done = semaphore("silu_done")
        split_done = semaphore("split_done")
        sq_done = semaphore("sq_done")
        std_done = semaphore("std_done")
        t_done = semaphore("t_done")
        t_ready = semaphore("t_ready")
        u2_done = semaphore("u2_done")
        x_done = semaphore("x_done")
        x_in = semaphore("x_in")
        y_done = semaphore("y_done")
        z_done = semaphore("z_done")
        zeros_done = semaphore("zeros_done")
        raw_in = [semaphore(f"raw_in{i}") for i in range(RAW)]
        bias_in = [semaphore(f"bias_in{i}") for i in range(2)]
        out_done = [semaphore(f"out_done{i}") for i in range(PR)]
        sems = {"split_done": split_done, "t_ready": t_ready, "lo_done": lo_done, "z_done": z_done, "exp_done": exp_done,
                "bias_done": bias_done, "x_done": x_done, "relu_done": relu_done, "std_done": std_done,
                "rope_done": rope_done, "ada_done": ada_done, "ada_part": ada_part,
                "ada_mm": ada_mm,
                "mix_done": mix_done}
        block = ctx.enter_context(nc.Block())

        def big_free(use):
            name, value = plan.big_free[use - 2]
            return sems[name], value

        def t_free(use):
            name, value = plan.t_free[use - 2]
            return sems[name], value

        def qk(slot, part):
            return arena[:, 2 * slot + part, :]

        vals = arena[:, 12:16, :].rearrange("p a b -> p (a b)").rearrange(
            "p (t h s d) -> p t h s d", t=6, h=HEADS, s=2)

        def ada_acc(s, v):
            k = 2 * s.par + v
            return pb[:, k, 0:ACOLS] if s.where == "pb" else gs[:, k * ACOLS:(k + 1) * ACOLS]

        def as32(ap):
            return ap.bitcast(F32)

        attns = [s for s in steps if s.kind == "attn"]
        group_no = {}
        for k, s in enumerate(attns):
            group_no[s.l, s.g] = k

        @block.sync
        def _(sp):
            for dst, src in ((vec[:, :, :], vecs), (gf[:, :], gfin), (cv[:, :, :], cvec),
                             (mt[:, :, :], mats), (mna[:, :], maskna)):
                sp.dma_start(dst, src).then_inc(const_in, 16)
            at = 0

            def blocks_until(n):
                nonlocal at
                while at < n:
                    name, l, idx = plan.raw[at]
                    if at >= RAW:
                        freed_by, value = plan.raw_free[at - RAW]
                        sp.wait_ge(sems[freed_by], value)
                    sp.dma_start(raw[:, at % RAW, :], dram[name][l, idx]).then_inc(raw_in[at % RAW], 16)
                    at += 1

            blocks_until(2)
            sp.dma_start(x[:, :, :], xt).then_inc(x_in, 16)
            for s in steps:
                blocks_until(s.loads)
                if s.kind == "in":
                    if s.first:
                        k = group_no[s.l, s.g]
                        if k:
                            sp.wait_ge(mix_done, attns[k - 1].mix[1])
                        if s.g == "A":
                            if s.l:
                                sp.wait_ge(ada_done, plan.ada_at[s.l, NADA - 1])
                            for h in range(2):
                                sp.dma_start(gs[:, h * 1024:(h + 1) * 1024], rpb[s.l, h]).then_inc(bias_in[h], 16)
                        if s.g == "C":
                            sp.dma_start(rt[:, :, :], rope[0]).then_inc(group_in, 16)
                            sp.dma_start(gs[:, 0:3 * P], masksw).then_inc(group_in, 16)
                        if s.g == "B":
                            sp.dma_start(rt[:, :, :], rope[1]).then_inc(group_in, 16)
                            sp.dma_start(gs[:, 0:768], wuq[s.l]).then_inc(group_in, 16)
                            sp.dma_start(gs[:, 768:1280], wukv[s.l]).then_inc(group_in, 16)
                if s.kind == "attn" and s.g == "A":
                    for h in range(2, HEADS):
                        sp.wait_ge(bias_done, max(u.bias[1] for u in s.units if u.h == h - 2 and u.biased))
                        sp.dma_start(gs[:, (h - 2) * 1024:(h - 1) * 1024], rpb[s.l, h]).then_inc(bias_in[h - 2], 16)
                if s.kind == "norm" and s.which == "final":
                    for k in range(KT):
                        sp.wait_ge(y_done, s.hs[k])
                        sp.dma_start(out[:, k, :], pb[:, k % PR, 0:S]).then_inc(out_done[k % PR], 16)
            for k in range(PR):
                sp.wait_ge(out_done[k], 16 * (KT // PR))

        @block.gpsimd
        def _(pool):
            def split_lo(b):
                pool.wait_ge(hi_split, b.i)
                sl = (b.i - 1) % WR
                pool.tensor_tensor(w_lo[:, sl, :], raw[:, b.n % RAW, :], as32(w_hi[:, sl, :]), ALU.subtract).then_inc(split_done, 1)

            for s in steps:
                if s.kind == "ssq" and s.pool:
                    pool.wait_ge(sq_done, s.sq)
                    if s.m:
                        if s.m > 1:
                            pool.wait_ge(acc_done, s.acc - 1)
                        pool.tensor_tensor(z[:, 2, 0:s.width], z[:, 2, 0:s.width], z[:, s.m % 2, 0:s.width], ALU.add).then_inc(acc_done, 1)
                for b in s.ahead:
                    split_lo(b)
                if s.kind == "attn" and s.g != "D":
                    width = TOK if s.l < DEPTH - 1 else S
                    if s.prev_out:
                        pool.wait_ge(big_ready, s.prev_out)
                    for t in range(2):
                        pool.wait_ge(osum_done, max(j.sum for j in s.jobs if j.h // 2 == t))
                        zz = z[:, t, 0:width]
                        pool.tensor_copy(mix_hi[:, t, 0:width], zz).then_inc(mix_half, 1)
                        pool.wait_ge(mix_half, s.mix[t])
                        pool.tensor_tensor(mix_lo[:, t, 0:width], zz, as32(mix_hi[:, t, 0:width]), ALU.subtract).then_inc(mix_done, 1)

        @block.scalar
        def _(act):
            def hi_copy(dst, src, value):
                act.activation(dst, src, ACT.Copy).then_inc(hi_done, 1)

            def rope_hi(s_hi, s_sum, src, slot, width):
                act.wait_ge(rope_done, s_sum)
                hi_copy(qk(slot, 0)[:, 0:width], src, s_hi)

            def rsqrt(dst, tmp, total, n, value):
                act.activation(tmp, total, ACT.Ln, bias=eps[:, :], scale=1.0 / n).then_inc(ln_done, 1)
                act.wait_ge(ln_done, value)
                act.activation(dst, tmp, ACT.Exp, scale=-0.5).then_inc(std_done, 1)

            def split_hi(b):
                act.wait_ge(raw_in[b.n % RAW], 16 * (b.n // RAW + 1))
                if b.before:
                    act.wait_ge(big_ready, b.before)
                act.activation(w_hi[:, (b.i - 1) % WR, :], raw[:, b.n % RAW, :], ACT.Copy).then_inc(hi_split, 1)

            act.wait_ge(const_in, 16 * 5)
            act.activation(amul[:, :, :], cv[:, :, :], ACT.Exp, scale=-1.0).then_inc(cexp_done, 1)
            act.wait_ge(x_in, 16)
            act.wait_ge(zeros_done, 2)
            for s in steps:
                for b in s.ahead:
                    split_hi(b)
                if s.kind == "ssq":
                    if s.after:
                        act.wait_ge(x_done, s.after)
                    if s.m >= 3:
                        act.wait_ge(acc_done, s.acc - 2)
                    dst = z[:, 2 if s.m == 0 else s.m % 2, 0:s.width]
                    act.activation(dst, x[:, s.m, 0:s.width], ACT.Square).then_inc(sq_done, 1)
                elif s.kind == "stat":
                    act.wait_ge(big_ready, s.br)
                    rsqrt(z[:, 1, 0:s.width], z[:, 0, 0:s.width], big[s.su % 2][:, 0:s.width], D, s.std)
                elif s.kind == "norm":
                    if s.which == "final":
                        continue
                    shift = 0 if s.which == "attn" else 3 * KT
                    for k in range(KT):
                        act.wait_ge(t_done, s.hs[k][0])
                        for v, (c0, n) in enumerate(segs(s.width)):
                            ins = act.activation(h_hi[:, k, c0:c0 + n], pb[:, k % PR, c0:c0 + n], ACT.Identity,
                                                 bias=ada[:, s.l, shift + k, v:v + 1])
                        ins.then_inc(hi_done, 1)
                elif s.kind == "in":
                    act.wait_ge(big_ready, s.br)
                    src = big[s.su % 2][:, 0:s.width]
                    if s.what in ("q", "k"):
                        hi_copy(qk(s.slot, 0)[:, 0:s.width], src, s.hi)
                    else:
                        for name, value in s.zwait:
                            act.wait_ge(sems[name], value)
                        act.activation(z[:, s.z, 0:s.width], src, ACT.Copy).then_inc(z_done, 1)
                elif s.kind == "vpost":
                    for p in s.pieces:
                        act.wait_ge(t_ready, p.tr)
                        src = tb[p.tu % 2][:, 0:p.n * P].rearrange("p (t h d) -> p t h d", t=p.n, h=2)
                        hi_copy(vals[:, p.kt:p.kt + p.n, 2 * s.slot:2 * s.slot + 2, 0, :], src, p.hi)
                elif s.kind == "rope":
                    rope_hi(s.hi, s.sum, z[:, s.z, 0:s.width], s.slot, s.width)
                elif s.kind == "bprep":
                    act.wait_ge(ada_done, s.ada_before)
                    act.wait_ge(z_done, s.zd)
                    act.activation(pb[:, 0, 0:s.wq], z[:, 0, 0:s.wq], ACT.Square).then_inc(sq_done, 1)
                    act.activation(pb[0:DH, 1, 0:s.wq], z[0:DH, 1, 0:s.wq], ACT.Square).then_inc(sq_done, 1)
                    act.activation(pb[:, 2, :], z[:, 2, :], ACT.Square).then_inc(sq_done, 1)
                    act.wait_ge(big_ready, s.ssq_q[1])
                    rsqrt(pb[:, 3, 0:s.wq], pb[:, 3, 0:s.wq], big[s.ssq_q[0] % 2][:, 0:s.wq], QLORA, s.std[0])
                    act.wait_ge(big_ready, s.ssq_kv[1])
                    rsqrt(pb[:, 0, :], pb[:, 0, :], big[s.ssq_kv[0] % 2][:, 0:TOK], KVLORA, s.std[1])
                    rope_hi(s.khl[0], s.krope, pb[:, 1, :], 5, TOK)
                    for t, (u, hl) in enumerate(s.q):
                        act.wait_ge(big_ready, u[1])
                        hi_copy(qk(t, 0)[:, 0:s.wq], big[u[0] % 2][:, 0:s.wq], hl[0])
                    act.wait_ge(big_ready, s.qr[1])
                    act.wait_ge(cn_done, s.cn[1])
                    act.activation(pb[:, 3, 0:s.wq], big[s.qr[0] % 2][:, 0:s.wq], ACT.Copy).then_inc(z_done, 1)
                    for t, (u, hl) in enumerate(s.k):
                        act.wait_ge(big_ready, u[1])
                        hi_copy(qk(3 + t, 0), big[u[0] % 2][:, 0:TOK], hl[0])
                    rope_hi(s.qhl[0], s.qrope, pb[:, 3, 0:s.wq], 2, s.wq)
                    for t, (u, hl) in enumerate(s.v):
                        act.wait_ge(t_ready, u[1])
                        hi_copy(vals[:, 2 * t:2 * t + 2, :, 0, :],
                                tb[u[0] % 2][:, :].rearrange("p (t h d) -> p t h d", t=2, h=HEADS), hl[0])
                elif s.kind == "attn":
                    sc = SCALE[s.g]
                    act.wait_ge(ada_done, s.ada_before)
                    if s.g == "D":
                        act.wait_ge(lam_dot, 2 * s.l + 2)
                        act.activation(lam[:, 2:4], lam[:, 0:2], ACT.Exp).then_inc(lam_exp, 1)
                    for i in range(len(s.units) + LAG + 1):
                        j = i - LAG - 1
                        if 0 <= j < len(s.units) and s.units[j].job.tiles[-1][0] == s.units[j].qt and s.units[j].last:
                            job = s.units[j].job
                            act.wait_ge(o_ready, job.ready)
                            if job.ou >= 2:
                                act.wait_ge(osum_done, plan.o_free[job.ou - 2])
                            act.activation(otmp[:, job.ou % 2, :], ob[job.ou % 2][DH:P, 0:2 * P], ACT.Copy).then_inc(half_done, 1)
                        j = i - LAG
                        if 0 <= j < len(s.units) and s.units[j].last:
                            u = s.units[j]
                            qc = (u.qt % 2) * P
                            k0 = s.jobs.index(u.job)
                            if k0:
                                act.wait_ge(o_ready, s.jobs[k0 - 1].ready)
                            for p in u.pieces[:1]:
                                act.wait_ge(t_ready, p.tr)
                                hi_copy(pt[:, 0, p.kt:p.kt + p.n, qc:qc + P],
                                        tb[p.tu % 2][:, 0:p.n * P].rearrange("p (t q) -> p t q", t=p.n), p.hi)
                        if i < len(s.units):
                            u = s.units[i]
                            c = col[:, u.un % 8, :]
                            pr = pb[:, u.un % PR, 0:u.w]
                            act.wait_ge(nmax_done, u.nm)
                            if i >= PR:
                                v = s.units[i - PR]
                                act.wait_ge(t_ready, (v if v.last else s.units[i - PR + 1]).pieces[-1].tr)
                            src = pr if u.biased else big[u.su % 2][:, S - u.wl:S + C]
                            ins = act.activation(pr, src, ACT.Exp, bias=c[:, NM:NM + 1], scale=sc, accum_out=c[:, L:L + 1])
                            if s.g == "C":
                                ins = act.activation(c[:, ES:ES + 1], vec[:, s.l, V_SINK + u.h:V_SINK + u.h + 1], ACT.Exp,
                                                     bias=c[:, NM:NM + 1])
                            ins.then_inc(exp_done, 1)
                        j = i - LAG
                        if 0 <= j < len(s.units) and s.units[j].last:
                            u = s.units[j]
                            qc = (u.qt % 2) * P
                            for p in u.pieces[1:]:
                                act.wait_ge(t_ready, p.tr)
                                hi_copy(pt[:, 0, p.kt:p.kt + p.n, qc:qc + P],
                                        tb[p.tu % 2][:, 0:p.n * P].rearrange("p (t q) -> p t q", t=p.n), p.hi)
                    if s.g == "D":
                        width = TOK if s.l < DEPTH - 1 else S
                        act.wait_ge(osum_done, s.end_sum)
                        for t, d in enumerate(s.dn):
                            act.activation(pb[:, t, 0:width], z[:, t, 0:width], ACT.Square).then_inc(sq_done, 1)
                        for t, d in enumerate(s.dn):
                            act.wait_ge(big_ready, d.br)
                            rsqrt(pb[:, t, 0:width], pb[:, t, 0:width], big[d.su % 2][:, 0:width], DH, d.std)
                        act.wait_ge(big_ready, s.prev_out)
                        for t, d in enumerate(s.dn):
                            act.wait_ge(cn_done, d.done)
                            act.activation(mix_hi[:, t, 0:width], z[:, t, 0:width], ACT.Copy).then_inc(mix_half, 1)
                elif s.kind == "up":
                    act.wait_ge(big_ready, s.br)
                    pa = pb[:, 2 * (s.c % 2), 0:s.width]
                    act.wait_ge(lo_done, s.lo - 2)
                    act.activation(pa, big[s.su % 2][:, 0:s.width], ACT.Relu).then_inc(relu_done, 1)
                    act.wait_ge(relu_done, s.relu)
                    act.activation(arena[:, s.c, 0:s.width], pa, ACT.Square).then_inc(hi_done, 1)

        @block.vector
        def _(dve):
            steps_done = [0]

            def link(ins):
                steps_done[0] += 1
                ins.then_inc(dve_step, 1)
                dve.wait_ge(dve_step, steps_done[0])

            def lo_sub(dst, src, hi, value, hi_value):
                dve.wait_ge(hi_done, hi_value)
                dve.tensor_tensor(dst, src, as32(hi), ALU.subtract).then_inc(lo_done, 1)

            def low(s, k):
                shift = 0 if s.which == "attn" else 3 * KT
                dve.wait_ge(hi_done, s.hs[k][1])
                for v, (c0, n) in enumerate(segs(s.width)):
                    ins = dve.scalar_tensor_tensor(out=h_lo[:, k, c0:c0 + n], in0=pb[:, k % PR, c0:c0 + n],
                                                   scalar=ada[:, s.l, shift + k, v:v + 1],
                                                   in1=as32(h_hi[:, k, c0:c0 + n]), op0=ALU.add, op1=ALU.subtract)
                ins.then_inc(lo_done, 1)

            link(dve.memset(eps[:, :], EPS))
            dve.memset(zeros[:, :], 0.0).then_inc(zeros_done, 1)
            dve.memset(col[:, :, :], 0.0).then_inc(zeros_done, 1)
            dve.wait_ge(zeros_done, 2)
            dve.wait_ge(cexp_done, 1)
            dve.wait_ge(const_in, 16 * 5)
            link(dve.tensor_scalar(amul[:, :, :], amul[:, :, :], 1.0, None, ALU.add))
            link(dve.reciprocal(amul[:, :, :], amul[:, :, :]))
            dve.tensor_tensor(cs[:, :, :], cv[:, :, :], amul[:, :, :], ALU.mult).then_inc(silu_done, 1)
            dve.wait_ge(silu_done, 1)
            n_bias = [0, 0]
            for s in steps:
                if s.kind == "ssq" and not s.pool:
                    dve.wait_ge(sq_done, s.sq)
                    if s.m:
                        if s.m > 1:
                            dve.wait_ge(acc_done, s.acc - 1)
                        dve.tensor_tensor(z[:, 2, 0:s.width], z[:, 2, 0:s.width], z[:, s.m % 2, 0:s.width], ALU.add).then_inc(acc_done, 1)
                elif s.kind == "ada":
                    dve.wait_ge(raw_in[s.n % RAW], 16 * (s.n // RAW + 1))
                    if s.kt:
                        dve.wait_ge(ada_part, s.part - 1)
                    elif s.lo_before:
                        dve.wait_ge(lo_done, s.lo_before)
                    for k in range(2):
                        for v in range(2):
                            acc, w, scalar = ada_acc(s, v), raw[:, s.n % RAW, k * ACOLS:(k + 1) * ACOLS], cs[:, s.kt + k, v:v + 1]
                            if s.kt + k == 0:
                                ins = dve.tensor_scalar(acc, w, scalar, None, ALU.mult)
                            else:
                                ins = dve.scalar_tensor_tensor(out=acc, in0=w, scalar=scalar, in1=acc, op0=ALU.mult, op1=ALU.add)
                        if k == 0:
                            link(ins)
                    ins.then_inc(ada_part, 1)
                elif s.kind == "adasum" or s.kind == "adamm" and s.last:
                    j0, n = s.j * (ACOLS // P), ACOLS // P
                    dve.wait_ge(t_ready, s.tr)
                    dve.tensor_tensor(ada[:, s.l, j0:j0 + n, :], tb[s.tu % 2][:, 0:2 * n].rearrange("p (m v) -> p m v", v=2),
                                      vec[:, s.l, V_BADA + j0:V_BADA + j0 + n].unsqueeze(2).broadcast_to([P, n, 2]),
                                      ALU.add).then_inc(ada_done, 1)
                elif s.kind == "norm":
                    dve.wait_ge(std_done, s.std)
                    if s.which != "final":
                        base = 0 if s.which == "attn" else 3 * KT
                        gcol = V_GATTN if s.which == "attn" else V_GMLP
                        dve.wait_ge(ada_done, max(plan.ada_at[s.l, base + j] for j in range(2 * KT)))
                        link(dve.scalar_tensor_tensor(out=amul[:, :, :], in0=ada[:, s.l, base + KT:base + 2 * KT, :], scalar=1.0,
                                                      in1=vec[:, s.l, gcol:gcol + KT].unsqueeze(2).broadcast_to([P, KT, 2]),
                                                      op0=ALU.add, op1=ALU.mult))
                    for k in range(KT):
                        if s.which == "final":
                            if k >= PR:
                                dve.wait_ge(out_done[k % PR], 16)
                            dve.scalar_tensor_tensor(out=pb[:, k % PR, 0:S], in0=x[:, k, 0:S], scalar=gf[:, k:k + 1],
                                                          in1=z[:, 1, 0:S], op0=ALU.mult, op1=ALU.mult).then_inc(y_done, 1)
                            continue
                        t, hi, lo = s.hs[k]
                        if k >= PR:
                            dve.wait_ge(lo_done, s.hs[k - PR][2])
                        for v, (c0, n) in enumerate(segs(s.width)):
                            ins = dve.scalar_tensor_tensor(out=pb[:, k % PR, c0:c0 + n], in0=x[:, k, c0:c0 + n],
                                                           scalar=amul[:, k, v:v + 1], in1=z[:, 1, c0:c0 + n],
                                                           op0=ALU.mult, op1=ALU.mult)
                        ins.then_inc(t_done, 1)
                        if k:
                            low(s, k - 1)
                    if s.which != "final":
                        low(s, KT - 1)
                elif s.kind == "in":
                    if s.what in ("q", "k"):
                        dve.wait_ge(big_ready, s.br)
                        lo_sub(qk(s.slot, 1)[:, 0:s.width], big[s.su % 2][:, 0:s.width], qk(s.slot, 0)[:, 0:s.width], s.lo, s.hi)
                elif s.kind == "vpost":
                    for p in s.pieces:
                        dve.wait_ge(t_ready, p.tr)
                        src = tb[p.tu % 2][:, 0:p.n * P].rearrange("p (t h d) -> p t h d", t=p.n, h=2)
                        v = vals[:, p.kt:p.kt + p.n, 2 * s.slot:2 * s.slot + 2]
                        lo_sub(v[:, :, :, 1, :], src, v[:, :, :, 0, :], p.lo, p.hi)
                elif s.kind == "rope":
                    zt = z[:, s.z, :]
                    dve.wait_ge(z_done, s.zd)
                    dve.wait_ge(group_in, 16 * s.gin)
                    dve_tmp = pb[:, 0, 0:S], pb[:, 1, 0:S]
                    dve.wait_ge(lo_done, s.lo - 1)
                    dve.tensor_tensor(dve_tmp[0], zt[:, 0:S], rt[:, 0, :], ALU.mult)
                    dve.wait_ge(t_ready, s.tr)
                    ins = dve.tensor_tensor(dve_tmp[1], tb[s.tu % 2][:, 0:S], rt[:, 1, :], ALU.mult)
                    ins.then_inc(rope_done, 1)
                    dve.wait_ge(rope_done, s.mul)
                    dve.tensor_tensor(zt[:, 0:S], dve_tmp[0], dve_tmp[1], ALU.add).then_inc(rope_done, 1)
                    dve.wait_ge(rope_done, s.sum)
                    lo_sub(qk(s.slot, 1)[:, 0:s.width], zt[:, 0:s.width], qk(s.slot, 0)[:, 0:s.width], s.lo, s.hi)
                elif s.kind == "bprep":
                    dve.wait_ge(group_in, 16 * s.gin)
                    dve.wait_ge(std_done, s.std[0])
                    dve.scalar_tensor_tensor(out=z[:, 0, 0:s.wq], in0=z[:, 0, 0:s.wq], scalar=vec[:, s.l, V_GQ:V_GQ + 1],
                                             in1=pb[:, 3, 0:s.wq], op0=ALU.mult, op1=ALU.mult)
                    dve.scalar_tensor_tensor(out=z[0:DH, 1, 0:s.wq], in0=z[0:DH, 1, 0:s.wq],
                                                  scalar=vec[0:DH, s.l, V_GQ + 1:V_GQ + 2], in1=pb[0:DH, 3, 0:s.wq],
                                                  op0=ALU.mult, op1=ALU.mult).then_inc(cn_done, 1)
                    dve.wait_ge(std_done, s.std[1])
                    dve.scalar_tensor_tensor(out=z[:, 2, :], in0=z[:, 2, :], scalar=vec[:, s.l, V_GKV:V_GKV + 1],
                                                  in1=pb[:, 0, :], op0=ALU.mult, op1=ALU.mult).then_inc(cn_done, 1)
                    dve.wait_ge(big_ready, s.rep[1])
                    dve.wait_ge(t_ready, s.krot[1])
                    rep = big[s.rep[0] % 2]
                    dve.tensor_tensor(pb[:, 1, 0:S], rep[:, 0:S], rt[:, 0, :], ALU.mult)
                    link(dve.tensor_tensor(pb[:, 2, 0:S], tb[s.krot[0] % 2][:, 0:S], rt[:, 1, :], ALU.mult))
                    dve.tensor_tensor(pb[:, 1, 0:S], pb[:, 1, 0:S], pb[:, 2, 0:S], ALU.add)
                    dve.tensor_copy(pb[:, 1, S:TOK], rep[:, S:TOK]).then_inc(rope_done, 1)
                    dve.wait_ge(rope_done, s.krope)
                    lo_sub(qk(5, 1), pb[:, 1, :], qk(5, 0), s.khl[1], s.khl[0])
                    for t, (u, hl) in enumerate(s.q):
                        dve.wait_ge(big_ready, u[1])
                        lo_sub(qk(t, 1)[:, 0:s.wq], big[u[0] % 2][:, 0:s.wq], qk(t, 0)[:, 0:s.wq], hl[1], hl[0])
                    for t, (u, hl) in enumerate(s.k):
                        dve.wait_ge(big_ready, u[1])
                        lo_sub(qk(3 + t, 1), big[u[0] % 2][:, 0:TOK], qk(3 + t, 0), hl[1], hl[0])
                    dve.wait_ge(z_done, s.qz)
                    dve.wait_ge(t_ready, s.qrot[1])
                    dve.tensor_tensor(pb[:, 0, 0:S], pb[:, 3, 0:S], rt[:, 0, :], ALU.mult)
                    dve.tensor_tensor(pb[:, 2, 0:S], tb[s.qrot[0] % 2][:, 0:S], rt[:, 1, :], ALU.mult).then_inc(rope_done, 1)
                    dve.wait_ge(rope_done, s.qmul)
                    dve.tensor_tensor(pb[:, 3, 0:S], pb[:, 0, 0:S], pb[:, 2, 0:S], ALU.add).then_inc(rope_done, 1)
                    dve.wait_ge(rope_done, s.qrope)
                    lo_sub(qk(2, 1)[:, 0:s.wq], pb[:, 3, 0:s.wq], qk(2, 0)[:, 0:s.wq], s.qhl[1], s.qhl[0])
                    for t, (u, hl) in enumerate(s.v):
                        dve.wait_ge(t_ready, u[1])
                        v = vals[:, 2 * t:2 * t + 2]
                        lo_sub(v[:, :, :, 1, :], tb[u[0] % 2][:, :].rearrange("p (t h d) -> p t h d", t=2, h=HEADS),
                               v[:, :, :, 0, :], hl[1], hl[0])
                elif s.kind == "attn":
                    sc = SCALE[s.g]
                    if s.g == "C":
                        link(dve.tensor_scalar(nsink[:, :], vec[:, s.l, V_SINK:V_SINK + HEADS], -1.0, None, ALU.mult))
                    if s.g == "D":
                        for t in range(2):
                            v = vec[:, s.l, V_LAM + 64 * t:V_LAM + 64 * t + 64]
                            dve.tensor_tensor_reduce(pb[:, t, 0:32], v[:, 0:32], v[:, 32:64], 1.0, 0.0, ALU.mult, ALU.add,
                                                     lam[:, t:t + 1]).then_inc(lam_dot, 1)
                        dve.wait_ge(lam_exp, s.l + 1)
                        link(dve.tensor_tensor(lam[:, 4:5], lam[:, 3:4], lam[:, 2:3], ALU.subtract))
                        link(dve.tensor_scalar(lam[:, 5:6], lam[:, 4:5], -LAM_INIT[s.l], None, ALU.add))
                        link(dve.tensor_scalar(dgain[:, :], vec[:, s.l, V_DNG:V_DNG + 1], 1.0 - LAM_INIT[s.l], None, ALU.mult))
                    for i in range(len(s.units) + LAG + 1):
                        if i < len(s.units):
                            u = s.units[i]
                            c = col[:, u.un % 8, :]
                            if u.biased:
                                if s.g == "A":
                                    if u.qt == 0:
                                        b = u.h % 2
                                        n_bias[b] += 1
                                        dve.wait_ge(bias_in[b], 16 * n_bias[b])
                                        tab = gs[:, b * 1024:(b + 1) * 1024].rearrange("p (e c) -> p e c", c=GRID_W)
                                        link(dve.scalar_tensor_tensor(
                                            out=tab, in0=tab, scalar=1.0 / sc,
                                            in1=mna[:, :].unsqueeze(1).broadcast_to([P, 1024 // GRID_W, GRID_W]),
                                            op0=ALU.mult, op1=ALU.add))
                                    off = (u.h % 2) * 1024 + (7 - 2 * u.qt) * GRID_W
                                    bias = gs[:, off:off + S]
                                else:
                                    off = P if u.qt == 0 else 0
                                    bias = gs[:, off:off + u.wl]
                                if i >= PR:
                                    dve.wait_ge(t_ready, s.units[i - PR].pieces[-1].tr)
                                dve.wait_ge(big_ready, u.br)
                                pr = pb[:, u.un % PR, :]
                                sl = big[u.su % 2]
                                dve.tensor_tensor_reduce(pr[:, 0:u.wl], sl[:, S - u.wl:S], bias, 1.0, LOWEST, ALU.add, ALU.max,
                                                              c[:, MX2:MX2 + 1]).then_inc(bias_done, 1)
                                dve.wait_ge(bias_done, u.bias[0])
                                dve.tensor_tensor_reduce(pr[:, u.wl:u.w], sl[:, S:S + C], zeros[:, :], 1.0, c[:, MX2:MX2 + 1],
                                                              ALU.add, ALU.max, c[:, MX:MX + 1]).then_inc(bias_done, 1)
                                dve.wait_ge(bias_done, u.bias[1])
                            else:
                                dve.wait_ge(big_ready, u.br)
                                link(dve.reduce_max(c[:, MX:MX + 1], big[u.su % 2][:, S - u.wl:S + C], AXX))
                            if s.g == "C":
                                ins = dve.tensor_scalar(c[:, NM:NM + 1], c[:, MX:MX + 1], -sc, nsink[:, u.h:u.h + 1],
                                                        ALU.mult, ALU.min)
                            else:
                                ins = dve.tensor_scalar(c[:, NM:NM + 1], c[:, MX:MX + 1], -sc, None, ALU.mult)
                            ins.then_inc(nmax_done, 1)
                        j = i - 1
                        if 0 <= j < len(s.units):
                            u = s.units[j]
                            c = col[:, u.un % 8, :]
                            dve.wait_ge(exp_done, u.exp)
                            if s.g == "C":
                                link(dve.tensor_tensor(c[:, L:L + 1], c[:, L:L + 1], c[:, ES:ES + 1], ALU.add))
                            dve.reciprocal(c[:, R:R + 1], c[:, L:L + 1]).then_inc(r_done, 1)
                            dve.wait_ge(r_done, u.r)
                            pr = pb[:, u.un % PR, 0:u.w]
                            if u.df is None:
                                dve.tensor_scalar(pr, pr, c[:, R:R + 1], None, ALU.mult).then_inc(pnorm_done, 1)
                            else:
                                link(dve.tensor_scalar(c[:, RL:RL + 1], c[:, R:R + 1], lam[:, 5:6], None, ALU.mult))
                                dve.wait_ge(pnorm_done, s.units[j - 1].pn)
                                dve.scalar_tensor_tensor(out=pr, in0=pr, scalar=c[:, RL:RL + 1],
                                                              in1=pb[:, (u.un - 1) % PR, 0:u.w], op0=ALU.mult, op1=ALU.add).then_inc(diff_done, 1)
                        j = i - LAG - 1
                        if 0 <= j < len(s.units) and s.units[j].job.tiles[-1][0] == s.units[j].qt and s.units[j].last:
                            job = s.units[j].job
                            dve.wait_ge(half_done, job.half)
                            dve.wait_ge(o_ready, job.ready)
                            r0 = DH * (job.h % 2)
                            dve.tensor_tensor(z[r0:r0 + DH, job.h // 2, 2 * P * job.qp:2 * P * (job.qp + 1)],
                                                   ob[job.ou % 2][0:DH, 0:2 * P], otmp[:, job.ou % 2, :], ALU.add).then_inc(osum_done, 1)
                        j = i - LAG
                        if 0 <= j < len(s.units) and s.units[j].last:
                            u = s.units[j]
                            qc = (u.qt % 2) * P
                            for p in u.pieces[:1]:
                                dve.wait_ge(t_ready, p.tr)
                                lo_sub(pt[:, 1, p.kt:p.kt + p.n, qc:qc + P],
                                       tb[p.tu % 2][:, 0:p.n * P].rearrange("p (t q) -> p t q", t=p.n),
                                       pt[:, 0, p.kt:p.kt + p.n, qc:qc + P], p.lo, p.hi)
                        j = i - LAG
                        if 0 <= j < len(s.units) and s.units[j].last:
                            u = s.units[j]
                            qc = (u.qt % 2) * P
                            for p in u.pieces[1:]:
                                dve.wait_ge(t_ready, p.tr)
                                lo_sub(pt[:, 1, p.kt:p.kt + p.n, qc:qc + P],
                                       tb[p.tu % 2][:, 0:p.n * P].rearrange("p (t q) -> p t q", t=p.n),
                                       pt[:, 0, p.kt:p.kt + p.n, qc:qc + P], p.lo, p.hi)
                    if s.g == "D":
                        width = TOK if s.l < DEPTH - 1 else S
                        dve.wait_ge(osum_done, s.end_sum)
                        for t, d in enumerate(s.dn):
                            dve.wait_ge(std_done, d.std)
                            dve.scalar_tensor_tensor(out=z[:, t, 0:width], in0=z[:, t, 0:width], scalar=dgain[:, 0:1],
                                                          in1=pb[:, t, 0:width], op0=ALU.mult, op1=ALU.mult).then_inc(cn_done, 1)
                        for t in range(2):
                            dve.wait_ge(mix_half, s.mix[t])
                            dve.tensor_tensor(mix_lo[:, t, 0:width], z[:, t, 0:width], as32(mix_hi[:, t, 0:width]),
                                              ALU.subtract).then_inc(mix_done, 1)
                elif s.kind in ("out", "down"):
                    uses = s.uses if s.kind == "out" else [s]
                    gate = 2 * KT if s.kind == "out" else 5 * KT
                    dve.wait_ge(ada_done, plan.ada_at[s.l, gate + KT - 1])
                    for u in uses:
                        dve.wait_ge(big_ready, u.br)
                        if u.x > KT:
                            dve.wait_ge(x_done, u.x - KT)
                        for v, (c0, n) in enumerate(segs(s.width)):
                            xs = x[:, u.m, c0:c0 + n]
                            ins = dve.scalar_tensor_tensor(out=xs, in0=big[u.su % 2][:, c0:c0 + n],
                                                           scalar=ada[:, s.l, gate + u.m, v:v + 1], in1=xs,
                                                           op0=ALU.mult, op1=ALU.add)
                        ins.then_inc(x_done, 1)
                elif s.kind == "up":
                    pa, pc = pb[:, 2 * (s.c % 2), 0:s.width], pb[:, 2 * (s.c % 2) + 1, 0:s.width]
                    dve.wait_ge(relu_done, s.relu)
                    dve.wait_ge(lo_done, s.lo - 2)
                    dve.tensor_tensor(pc, pa, pa, ALU.mult).then_inc(u2_done, 1)
                    dve.wait_ge(u2_done, s.u2)
                    lo_sub(arena[:, CPQ + s.c, 0:s.width], pc, arena[:, s.c, 0:s.width], s.lo, s.hi)

        @block.tensor
        def _(pe):
            def mm(dst, lhs, rhs, start, stop):
                return pe.matmul(dst, lhs, rhs, start=start, stop=stop)

            def dense_pair(s, act_hi, act_lo):
                for k in range(KT):
                    pe.wait_ge(lo_done, s.hs[k][2])
                    for u in (s, s.pair):
                        if k == 0:
                            pe.wait_ge(split_done, u.b.i)
                            if u.su >= 2:
                                pe.wait_ge(*big_free(u.su))
                        for p, (w, a) in enumerate(((w_hi, act_hi), (w_hi, act_lo), (w_lo, act_hi))):
                            for c0, m in segs(u.width):
                                ins = mm(big[u.su % 2][:, c0:c0 + m], w[:, (u.b.i - 1) % WR, k * P:(k + 1) * P],
                                         a[:, k, c0:c0 + m], k == 0 and p == 0, k == KT - 1 and p == 2)
                        if k == KT - 1:
                            ins.then_inc(big_ready, 1)

            def dense(dst, wsl, act_hi, act_lo, ks, wcols, width, need=None):
                n = len(ks)
                for i, k in enumerate(ks):
                    if need is not None:
                        pe.wait_ge(lo_done, need[i])
                    wc = wcols(k)
                    for p, (w, a) in enumerate(((w_hi, act_hi), (w_hi, act_lo), (w_lo, act_hi))):
                        for c0, m in segs(width):
                            ins = mm(dst[:, c0:c0 + m], w[:, wsl, wc:wc + P], a(k)[:, c0:c0 + m],
                                     i == 0 and p == 0, i == n - 1 and p == 2)
                return ins

            def plain(dst, terms, width):
                for c0, m in segs(width):
                    for i, (w, a) in enumerate(terms):
                        ins = mm(dst[:, c0:c0 + m], w, a[:, c0:c0 + m], i == 0, i == len(terms) - 1)
                return ins

            def mat(i):
                return mt[:, i, :]

            def b_prep(s):
                pe.wait_ge(group_in, 16 * s.gin)
                uq = gs[:, 0:768].rearrange("p (k c) -> p k c", k=2)
                ukv = gs[:, 768:1280]
                pe.wait_ge(sq_done, s.sq[1])
                if s.ssq_q[0] >= 2:
                    pe.wait_ge(*big_free(s.ssq_q[0]))
                plain(big[s.ssq_q[0] % 2], [(mat(M_ONES), pb[:, 0, :]), (mat(M_ONES)[0:DH], pb[0:DH, 1, :])], s.wq).then_inc(big_ready, 1)
                pe.wait_ge(sq_done, s.sq[2])
                if s.ssq_kv[0] >= 2:
                    pe.wait_ge(*big_free(s.ssq_kv[0]))
                plain(big[s.ssq_kv[0] % 2], [(mat(M_ONES), pb[:, 2, :])], TOK).then_inc(big_ready, 1)
                r = slice(DH, DH + ROPE)
                if s.rep[0] >= 2:
                    pe.wait_ge(*big_free(s.rep[0]))
                plain(big[s.rep[0] % 2], [(mat(M_REP)[r], z[r, 1, :])], TOK).then_inc(big_ready, 1)
                if s.krot[0] >= 2:
                    pe.wait_ge(*t_free(s.krot[0]))
                plain(tb[s.krot[0] % 2], [(mat(M_RROT)[r], z[r, 1, :])], S).then_inc(t_ready, 1)
                pe.wait_ge(cn_done, s.cn[0])
                for t, u in enumerate([s.q[0][0], s.q[1][0], s.qr]):
                    if u[0] >= 2:
                        pe.wait_ge(*big_free(u[0]))
                    c = slice(t * P, (t + 1) * P)
                    plain(big[u[0] % 2], [(uq[:, 0, c], z[:, 0, :]), (uq[0:DH, 1, c], z[0:DH, 1, :])], s.wq).then_inc(big_ready, 1)
                pe.wait_ge(cn_done, s.cn[1])
                for t, (u, _) in enumerate(s.k):
                    if u[0] >= 2:
                        pe.wait_ge(*big_free(u[0]))
                    plain(big[u[0] % 2], [(ukv[:, t * P:(t + 1) * P], z[:, 2, :])], TOK).then_inc(big_ready, 1)
                pe.wait_ge(z_done, s.qz)
                if s.qrot[0] >= 2:
                    pe.wait_ge(*t_free(s.qrot[0]))
                plain(tb[s.qrot[0] % 2], [(mat(M_P32), pb[:, 3, :])], S).then_inc(t_ready, 1)
                for t, (u, _) in enumerate(s.v):
                    if u[0] >= 2:
                        pe.wait_ge(*t_free(u[0]))
                    for j in range(2):
                        c = (2 * t + j) * P
                        ins = mm(tb[u[0] % 2][:, j * 256:(j + 1) * 256], z[:, 2, c:c + P], ukv[:, 256:512], True, True)
                    ins.then_inc(t_ready, 1)

            def operands(g, h, t):
                if g == "A":
                    return [(h // 2, 2 + h // 2, slice(DH * (h % 2), DH * (h % 2) + DH))]
                if g == "C":
                    return [(h % 2, 2, slice(DH * (h // 2), DH * (h // 2) + DH))]
                if g == "B":
                    return [(h // 2, 3 + h // 2, slice(DH * (h % 2), DH * (h % 2) + DH)),
                            (2, 5, slice(ROPE * h, ROPE * h + ROPE))]
                c = 2 * h + t
                return [(c // 4, 2 + c // 4, slice(32 * (c % 4), 32 * (c % 4) + 32))]

            def transposes(u, pieces):
                if u.df:
                    pe.wait_ge(diff_done, u.df)
                else:
                    pe.wait_ge(pnorm_done, u.pn)
                for p in pieces:
                    if p.tu >= 2:
                        pe.wait_ge(*t_free(p.tu))
                    for n in range(p.n):
                        c = p.col + n * P
                        ins = pe.transpose(tb[p.tu % 2][:, n * P:(n + 1) * P], pb[:, u.un % PR, c:c + P], mat(M_ID))
                    ins.then_inc(t_ready, 1)

            def values(s, u):
                job = u.job
                pe.wait_ge(lo_done, u.pieces[-1].lo)
                if job.ou >= 2:
                    pe.wait_ge(osum_done, plan.o_free[job.ou - 2])
                hv = job.h // 2 if s.g == "C" else job.h
                kts = [4, 5] + sorted({k for _, loc in job.tiles for k in loc})
                for n, kt in enumerate(kts):
                    cols = [qt % 2 for qt, loc in job.tiles if kt >= 4 or kt in loc]
                    c = slice(cols[0] * P, (cols[-1] + 1) * P)
                    for part in range(2):
                        ins = mm(ob[job.ou % 2][:, c], vals[:, kt, hv, :, :].rearrange("p s d -> p (s d)"),
                                 pt[:, part, kt, c], n == 0 and part == 0, n == len(kts) - 1 and part == 1)
                ins.then_inc(o_ready, 1)

            def attn(s):
                pe.wait_ge(lo_done, s.qlo)
                for i in range(len(s.units) + LAG + 1):
                    if i < len(s.units):
                        u = s.units[i]
                        if u.su >= 2:
                            pe.wait_ge(*big_free(u.su))
                        q = slice(u.qt * P, (u.qt + 1) * P)
                        parts = [(S, S + C, S)] + ([(S - u.wl, S, u.loc[0] * P)] if u.loc else [])
                        for a, b, k0 in parts:
                            ops = [(qk(qs, qp)[r, q], qk(ks, kp)[r, k0:k0 + b - a])
                                   for qs, ks, r in operands(s.g, u.h, u.t) for qp, kp in ((0, 0), (1, 0), (0, 1))]
                            for n, (w, m) in enumerate(ops):
                                ins = mm(big[u.su % 2][:, a:b], w, m, n == 0, n == len(ops) - 1)
                        ins.then_inc(big_ready, 1)
                    j = i - LAG
                    transposed = s.units[j] if 0 <= j < len(s.units) and s.units[j].last else None
                    if transposed:
                        transposes(transposed, transposed.pieces[:1])
                    j = i - LAG - 1
                    if 0 <= j < len(s.units) and s.units[j].job.tiles[-1][0] == s.units[j].qt and s.units[j].last:
                        values(s, s.units[j])
                    if transposed:
                        transposes(transposed, transposed.pieces[1:])
                if s.g == "D":
                    for t, d in enumerate(s.dn):
                        width = TOK if s.l < DEPTH - 1 else S
                        pe.wait_ge(sq_done, d.sq)
                        if d.su >= 2:
                            pe.wait_ge(*big_free(d.su))
                        plain(big[d.su % 2], [(mat(M_BONES), pb[:, t, :])], width).then_inc(big_ready, 1)

            pe.wait_ge(const_in, 16 * 5)
            for s in steps:
                if s.kind == "adamm":
                    pe.wait_ge(raw_in[s.n % RAW], 16 * (s.n // RAW + 1))
                    if s.kt == 0:
                        pe.wait_ge(silu_done, 1)
                        if s.tu >= 2:
                            pe.wait_ge(*t_free(s.tu))
                    for k in range(2):
                        for m in range(ACOLS // P):
                            c = k * ACOLS + m * P
                            ins = mm(tb[s.tu % 2][:, 2 * m:2 * m + 2], raw[:, s.n % RAW, c:c + P], cs[:, s.kt + k, :],
                                     c == s.kt == 0, s.kt + k == KT - 1 and m == ACOLS // P - 1)
                    if s.last:
                        ins.then_inc(t_ready, 1)
                    else:
                        ins.then_inc(ada_mm, 1)
                elif s.kind == "adasum":
                    pe.wait_ge(ada_part, s.part)
                    if s.tu >= 2:
                        pe.wait_ge(*t_free(s.tu))
                    for m in range(ACOLS // P):
                        for v in range(2):
                            ins = mm(tb[s.tu % 2][:, 2 * m + v:2 * m + v + 1], ada_acc(s, v)[:, m * P:(m + 1) * P],
                                     mat(M_ONES)[:, 0:1], True, True)
                    ins.then_inc(t_ready, 1)
                elif s.paired:
                    continue
                elif s.pair is not None:
                    dense_pair(s, h_hi, h_lo)
                elif s.kind == "stat":
                    pe.wait_ge(acc_done, s.acc)
                    if s.su >= 2:
                        pe.wait_ge(*big_free(s.su))
                    plain(big[s.su % 2], [(mat(M_ONES), z[:, 2, :])], s.width).then_inc(big_ready, 1)
                elif s.kind == "in":
                    pe.wait_ge(split_done, s.b.i)
                    if s.su >= 2:
                        pe.wait_ge(*big_free(s.su))
                    ins = dense(big[s.su % 2], (s.b.i - 1) % WR, lambda k: h_hi[:, k, :], lambda k: h_lo[:, k, :], range(KT),
                                lambda k: k * P, s.width, [hh[2] for hh in s.hs])
                    ins.then_inc(big_ready, 1)
                elif s.kind == "vpost":
                    pe.wait_ge(z_done, s.zd)
                    for p in s.pieces:
                        if p.tu >= 2:
                            pe.wait_ge(*t_free(p.tu))
                        for j in range(p.n):
                            kt = p.kt + j
                            ins = pe.transpose(tb[p.tu % 2][:, j * P:(j + 1) * P], z[:, s.z, kt * P:(kt + 1) * P], mat(M_ID))
                        ins.then_inc(t_ready, 1)
                elif s.kind == "rope":
                    pe.wait_ge(z_done, s.zd)
                    if s.tu >= 2:
                        pe.wait_ge(*t_free(s.tu))
                    plain(tb[s.tu % 2], [(mat(M_P64 if s.g == "C" else M_P32), z[:, s.z, :])], S).then_inc(t_ready, 1)
                elif s.kind == "bprep":
                    b_prep(s)
                elif s.kind == "attn":
                    attn(s)
                elif s.kind == "out":
                    pe.wait_ge(split_done, s.b.i)
                    pe.wait_ge(mix_done, s.mix)
                    for k, u in enumerate(s.uses):
                        if u.su >= 2:
                            pe.wait_ge(*big_free(u.su))
                        ins = dense(big[u.su % 2], (s.b.i - 1) % WR, lambda kk: mix_hi[:, kk, :], lambda kk: mix_lo[:, kk, :],
                                    range(2), lambda kk: kk * 4 * P + k * P, s.width)
                        ins.then_inc(big_ready, 1)
                elif s.kind == "up":
                    pe.wait_ge(split_done, s.b.i)
                    if s.su >= 2:
                        pe.wait_ge(*big_free(s.su))
                    ins = dense(big[s.su % 2], (s.b.i - 1) % WR, lambda k: h_hi[:, k, :], lambda k: h_lo[:, k, :], range(KT),
                                lambda k: k * P, s.width, [hh[2] for hh in s.hs])
                    ins.then_inc(big_ready, 1)
                elif s.kind == "down":
                    pe.wait_ge(split_done, s.b.i)
                    if s.su >= 2:
                        pe.wait_ge(*big_free(s.su))
                    ins = dense(big[s.su % 2], (s.b.i - 1) % WR, lambda k: arena[:, k, :], lambda k: arena[:, CPQ + k, :],
                                range(CPQ), lambda k: k * P, s.width, s.us)
                    ins.then_inc(big_ready, 1)



def _matrices():
    m = np.zeros((P, 7, P), np.float32)
    m[:, M_ID] = np.eye(P)
    m[:, M_ONES] = 1.0
    m[:, M_BONES] = np.kron(np.eye(2), np.ones((DH, DH)))

    def rot(n):
        r = np.zeros((n, n), np.float32)
        for d in range(n // 2):
            r[d + n // 2, d] = -1.0
            r[d, d + n // 2] = 1.0
        return r

    m[:, M_P64] = np.kron(np.eye(2), rot(64))
    m[:, M_P32] = np.kron(np.eye(4), rot(32))
    m[DH:DH + ROPE, M_REP] = np.tile(np.eye(ROPE), (1, HEADS))
    m[DH:DH + ROPE, M_RROT] = np.tile(rot(ROPE), (1, HEADS))
    return m


def _rope_table(dim):
    nf = dim // 4
    freqs = (np.float32(ROPE_BASE) ** (-np.arange(nf, dtype=np.float32) / np.float32(nf))).astype(np.float32)
    t = np.arange(S)
    row, column = (t // GRID_W).astype(np.float32), (t % GRID_W).astype(np.float32)
    ang = np.concatenate([row[:, None] * freqs, column[:, None] * freqs], axis=1).astype(np.float32)
    f = np.arange(P) % (dim // 2)
    return np.stack([np.cos(ang)[:, f].T, np.sin(ang)[:, f].T], axis=1).astype(np.float32)


def _column_mask():
    qc = np.arange(P) % GRID_W
    c0 = np.clip(qc - NA_COLS // 2, 0, GRID_W - NA_COLS)[:, None]
    kc = np.arange(GRID_W)[None, :]
    return np.where((kc >= c0) & (kc < c0 + NA_COLS), 0.0, NEG).astype(np.float32)


def _window_mask():
    q, k = np.arange(P)[:, None], np.arange(P)[None, :]
    return np.concatenate([np.where(k >= q, 0.0, NEG), np.zeros((P, P)), np.where(k <= q, 0.0, NEG)], axis=1).astype(np.float32)



def _cols(v):
    return v.reshape(-1, P).T


def _vectors(b_ada, norm_attn_g, norm_mlp_g, mla_q_norm_g, mla_kv_norm_g, diff_norm_g, swa_sink, diff_lambda):
    v = np.zeros((P, DEPTH, V_LEN), np.float32)
    for l in range(DEPTH):
        v[:, l, V_BADA:V_BADA + NADA] = _cols(b_ada[l])
        v[:, l, V_GATTN:V_GATTN + KT] = _cols(norm_attn_g[l])
        v[:, l, V_GMLP:V_GMLP + KT] = _cols(norm_mlp_g[l])
        v[:, l, V_GQ] = mla_q_norm_g[l, 0:P]
        v[0:QLORA - P, l, V_GQ + 1] = mla_q_norm_g[l, P:]
        v[:, l, V_GKV] = mla_kv_norm_g[l]
        v[:, l, V_DNG] = np.concatenate([diff_norm_g[l]] * 2)
        v[:, l, V_SINK:V_SINK + HEADS] = swa_sink[l][None, :]
        v[:, l, V_LAM:V_LAM + 128] = diff_lambda[l].reshape(1, -1)
    return v


def _w_in_blocks(w):
    a, b, c, d = 0, 768, 1120, 1632
    order = list(range(a, a + 768))
    order += list(range(b, b + QLORA)) + list(range(b + 320, b + 352)) + [-1] * 32 + list(range(b + QLORA, b + 320))
    for h in (0, 2, 1, 3):
        order += list(range(c + DH * h, c + DH * (h + 1)))
    order += list(range(c + 256, c + 512)) + list(range(d, d + 768))
    padded = np.concatenate([w, np.zeros_like(w[:, :, :1])], axis=2)
    return np.ascontiguousarray(
        padded[:, :, order].reshape(DEPTH, KT, P, NIN, P).transpose(0, 3, 2, 1, 4)).reshape(DEPTH, NIN, P, D)


def _blocks(w, n):
    return np.ascontiguousarray(w.reshape(DEPTH, KT, P, n, P).transpose(0, 3, 2, 1, 4)).reshape(DEPTH, n, P, D)


def _rpb_windows(rpb):
    qc, kc = np.arange(GRID_W)[:, None], np.arange(GRID_W)[None, :]
    dc = np.clip(kc - qc + NA_COLS - 1, 0, 2 * NA_COLS - 2)
    win = rpb[:, :, :, dc].transpose(0, 1, 3, 2, 4)
    pad = np.zeros_like(win[:, :, :, :1])
    both = np.stack([np.concatenate([win, pad], axis=3), np.concatenate([pad, win], axis=3)], axis=2)
    return np.ascontiguousarray(both).reshape(DEPTH, HEADS, P, 1024)


def kernel(x, c, ctx, c_ctx, w_ada, b_ada, norm_attn_g, w_in, na_rpb, mla_q_norm_g, mla_w_uq, mla_kv_norm_g, mla_w_ukv,
           swa_sink, diff_lambda, diff_norm_g, w_out, norm_mlp_g, w_up, w_down, final_norm_g):
    import concourse.bacc as bacc
    from concourse.bass_utils import run_bass_kernel_spmd

    a = {k: np.asarray(v) for k, v in dict(
        x=x, c=c, ctx=ctx, c_ctx=c_ctx, w_ada=w_ada, b_ada=b_ada, norm_attn_g=norm_attn_g, w_in=w_in, na_rpb=na_rpb,
        mla_q_norm_g=mla_q_norm_g, mla_w_uq=mla_w_uq, mla_kv_norm_g=mla_kv_norm_g, mla_w_ukv=mla_w_ukv, swa_sink=swa_sink,
        diff_lambda=diff_lambda, diff_norm_g=diff_norm_g, w_out=w_out, norm_mlp_g=norm_mlp_g, w_up=w_up, w_down=w_down,
        final_norm_g=final_norm_g).items()}
    tokens = np.concatenate([a["x"][0], a["ctx"][0]], axis=0)
    nope = [h * 96 + i for h in range(HEADS) for i in range(DH)]
    rope = [h * 96 + DH + i for h in range(HEADS) for i in range(ROPE)]
    uq = np.concatenate([a["mla_w_uq"], np.zeros((DEPTH, 2 * P - QLORA, 384), np.float32)], axis=1)[:, :, nope + rope]
    kcols = [h * P + i for h in range(HEADS) for i in range(DH)]
    vcols = [h * P + DH + i for h in range(HEADS) for i in range(DH)]
    wo = a["w_out"].reshape(DEPTH, 4, 2, P, 2, 4, P)
    arrays = {
        "xt": tokens.T.reshape(KT, P, TOK).transpose(1, 0, 2),
        "cvec": np.stack([_cols(a["c"][0]), _cols(a["c_ctx"])], axis=2),
        "vecs": _vectors(a["b_ada"], a["norm_attn_g"], a["norm_mlp_g"], a["mla_q_norm_g"], a["mla_kv_norm_g"],
                         a["diff_norm_g"], a["swa_sink"], a["diff_lambda"]),
        "gfin": _cols(a["final_norm_g"]),
        "mats": _matrices(),
        "rope": np.stack([_rope_table(64), _rope_table(32)]),
        "maskna": _column_mask(),
        "masksw": _window_mask(),
        "rpb": _rpb_windows(a["na_rpb"]),
        "wuq": uq.reshape(DEPTH, 2, P, 384).transpose(0, 2, 1, 3).reshape(DEPTH, P, 768),
        "wukv": a["mla_w_ukv"][:, :, kcols + vcols],
        "w_ada": a["w_ada"].reshape(DEPTH, AKB, 2, P, AHC, ACOLS).transpose(0, 4, 1, 3, 2, 5).reshape(DEPTH, AHC * AKB, P, D),
        "w_in": _w_in_blocks(a["w_in"]),
        "w_out": wo.transpose(0, 1, 4, 3, 2, 5, 6).reshape(DEPTH, 8, P, D),
        "w_up": _blocks(a["w_up"], NCHUNK),
        "w_down": a["w_down"].reshape(DEPTH, NQ, CPQ, P, KT, P).transpose(0, 1, 4, 3, 2, 5).reshape(DEPTH, NQ * KT, P, D),
    }
    arrays = {k: np.ascontiguousarray(v) for k, v in arrays.items()}
    nc = bacc.Bacc("TRN2", target_bir_lowering=False, num_devices=1, dynamic_dma_scratch_size=1024)
    args = {k: nc.dram_tensor(k + "_dram", v.shape, F32, kind="ExternalInput").ap() for k, v in arrays.items()}
    out = nc.dram_tensor("out_dram", (P, KT, S), F32, kind="ExternalOutput").ap()
    build_program(nc, out=out, **args)
    r = run_bass_kernel_spmd(nc, [{k + "_dram": v for k, v in arrays.items()}], core_ids=[0])
    got = r.results[0]["out_dram"]
    return got.transpose(2, 1, 0).reshape(1, S, D)
```
